# Optimizing a Trainium2 kernel written in Bass

```python
import math
import jax
import jax.numpy as jnp
from jax import lax
import numpy as np
import jax, jax.numpy as jnp

D_MODEL = 1024
BATCH = 1
SEQ = 256
DEPTH = 4

N_MIXERS = 3
ROPE_THETA = 500000.0
EPS = 1e-6
Q_BLOCK = 128
MASK_VALUE = -1e30

A_HEADS = 8
A_HEAD_DIM = D_MODEL // A_HEADS // 2
A_V_DIM = 2 * A_HEAD_DIM
A_ROT = A_HEAD_DIM // 4

B_HEADS = 16
B_Q_RANK = 384
B_KV_RANK = 256
B_NOPE = 64
B_ROPE = 32
B_V = 64

C_GROUPS = ((128, 1), (512, 4), (2048, 16))
C_HEADS = 16
C_HEAD_DIM = 64
C_ROT = C_HEAD_DIM // 4
C_BLOCK = 64

FFN_DIM = -(-8 * D_MODEL // (3 * 256)) * 256

N_A = (DEPTH + 2) // 3
N_B = (DEPTH + 1) // 3
N_C = DEPTH // 3


def rms_norm(x, g):
    xf = x.astype(jnp.float32)
    y = xf * lax.rsqrt(jnp.mean(xf * xf, axis=-1, keepdims=True) + EPS) * g.astype(jnp.float32)
    return y.astype(x.dtype)

def rope_tables(seq_len, rot_dim):
    pos = jnp.arange(seq_len, dtype=jnp.float32)
    inv = ROPE_THETA ** (-jnp.arange(0, rot_dim, 2, dtype=jnp.float32) / rot_dim)
    ang = pos[:, None] * inv[None, :]
    return jnp.cos(ang), jnp.sin(ang)

def apply_rope(x, cos, sin):
    r = cos.shape[-1]
    shape = (x.shape[1],) + (1,) * (x.ndim - 3) + (r,)
    c = cos.reshape(shape)
    s = sin.reshape(shape)
    xf = x[..., :2 * r].astype(jnp.float32)
    x1, x2 = xf[..., :r], xf[..., r:]
    rot = jnp.concatenate([x1 * c - x2 * s, x2 * c + x1 * s], axis=-1).astype(x.dtype)
    return jnp.concatenate([rot, x[..., 2 * r:]], axis=-1)

def _to_blocks(t):
    b, h, s, d = t.shape
    return t.reshape(b, h, s // Q_BLOCK, Q_BLOCK, d).transpose(2, 0, 1, 3, 4)

def _from_blocks(t):
    nb, b, h, q, d = t.shape
    return t.transpose(1, 2, 0, 3, 4).reshape(b, h, nb * q, d)

def diff_attention(h, w_qkv, lam_q1, lam_k1, lam_q2, lam_k2, subln, w_o, lambda_init, cos, sin):
    B, S, _ = h.shape
    qk_w = 2 * A_HEADS * A_HEAD_DIM
    qkv = h @ w_qkv
    q = qkv[..., :qk_w].reshape(B, S, 2 * A_HEADS, A_HEAD_DIM)
    k = qkv[..., qk_w:2 * qk_w].reshape(B, S, 2 * A_HEADS, A_HEAD_DIM)
    v = qkv[..., 2 * qk_w:].reshape(B, S, A_HEADS, A_V_DIM)
    q = (apply_rope(q, cos, sin) * (A_HEAD_DIM ** -0.5)).transpose(0, 2, 1, 3)
    k = apply_rope(k, cos, sin).transpose(0, 2, 1, 3)
    v = v.transpose(0, 2, 1, 3)
    lam = (jnp.exp(jnp.sum(lam_q1.astype(jnp.float32) * lam_k1.astype(jnp.float32)))
           - jnp.exp(jnp.sum(lam_q2.astype(jnp.float32) * lam_k2.astype(jnp.float32)))
           + lambda_init)

    def block(qb):
        s = jnp.einsum('bhqd,bhkd->bhqk', qb, k).astype(jnp.float32)
        p = jax.nn.softmax(s, axis=-1).reshape(B, A_HEADS, 2, qb.shape[2], S)
        a = p[:, :, 0] - lam * p[:, :, 1]
        return jnp.einsum('bhqk,bhkd->bhqd', a.astype(v.dtype), v)

    o = _from_blocks(lax.map(block, _to_blocks(q)))
    o = rms_norm(o, subln) * (1.0 - lambda_init)
    o = o.transpose(0, 2, 1, 3).reshape(B, S, A_HEADS * A_V_DIM)
    return o @ w_o

def latent_attention(h, w_a, q_norm, kv_norm, w_qb, w_kvb, w_o, cos, sin):
    B, S, _ = h.shape
    a = h @ w_a
    q_lat = rms_norm(a[..., :B_Q_RANK], q_norm)
    kv_lat = rms_norm(a[..., B_Q_RANK:B_Q_RANK + B_KV_RANK], kv_norm)
    k_rope = apply_rope(a[..., B_Q_RANK + B_KV_RANK:], cos, sin)
    scale = (B_NOPE + B_ROPE) ** -0.5
    q = (q_lat @ w_qb).reshape(B, S, B_HEADS, B_NOPE + B_ROPE)
    q_nope = (q[..., :B_NOPE] * scale).transpose(0, 2, 1, 3)
    q_rope = (apply_rope(q[..., B_NOPE:], cos, sin) * scale).transpose(0, 2, 1, 3)
    kv = (kv_lat @ w_kvb).reshape(B, S, B_HEADS, B_NOPE + B_V)
    k_nope = kv[..., :B_NOPE].transpose(0, 2, 1, 3)
    v = kv[..., B_NOPE:].transpose(0, 2, 1, 3)

    def block(qs):
        qn, qr = qs
        s = (jnp.einsum('bhqd,bhkd->bhqk', qn, k_nope)
             + jnp.einsum('bhqr,bkr->bhqk', qr, k_rope)).astype(jnp.float32)
        p = jax.nn.softmax(s, axis=-1)
        return jnp.einsum('bhqk,bhkd->bhqd', p.astype(v.dtype), v)

    o = _from_blocks(lax.map(block, (_to_blocks(q_nope), _to_blocks(q_rope))))
    o = o.transpose(0, 2, 1, 3).reshape(B, S, B_HEADS * B_V)
    return o @ w_o

def _dilated_group(q, k, v, window, dilation):
    B, S, H, hd = q.shape
    radius = (window // 2) // dilation
    L = S // dilation
    nb = -(-L // C_BLOCK)
    Lp = nb * C_BLOCK

    def phase(t):
        t = t.reshape(B, L, dilation, H, hd).transpose(0, 2, 3, 1, 4)
        return jnp.pad(t, ((0, 0), (0, 0), (0, 0), (0, Lp - L), (0, 0)))

    def band(t):
        t = jnp.pad(phase(t), ((0, 0), (0, 0), (0, 0), (C_BLOCK, C_BLOCK), (0, 0)))
        t = t.reshape(B, dilation, H, nb + 2, C_BLOCK, hd)
        return jnp.concatenate([t[:, :, :, :-2], t[:, :, :, 1:-1], t[:, :, :, 2:]], axis=-2)

    qb = phase(q).reshape(B, dilation, H, nb, C_BLOCK, hd)
    kb, vb = band(k), band(v)
    blk = jnp.arange(nb)[:, None]
    qpos = blk * C_BLOCK + jnp.arange(C_BLOCK)[None, :]
    kpos = (blk - 1) * C_BLOCK + jnp.arange(3 * C_BLOCK)[None, :]
    mask = ((jnp.abs(qpos[:, :, None] - kpos[:, None, :]) <= radius)
            & (kpos[:, None, :] >= 0) & (kpos[:, None, :] < L))
    s = jnp.einsum('bphnqd,bphnkd->bphnqk', qb, kb).astype(jnp.float32)
    s = jnp.where(mask, s, MASK_VALUE)
    lse = jax.nn.logsumexp(s, axis=-1, keepdims=True)
    p = jnp.exp(s - lse)
    o = jnp.einsum('bphnqk,bphnkd->bphnqd', p.astype(v.dtype), vb)
    o = o.reshape(B, dilation, H, Lp, hd)[:, :, :, :L].transpose(0, 3, 1, 2, 4).reshape(B, S, H, hd)
    lse = lse[..., 0].reshape(B, dilation, H, Lp)[..., :L].transpose(0, 3, 1, 2).reshape(B, S, H)
    return o, lse

def dilated_attention(h, w_qkv, w_o, cos, sin):
    B, S, _ = h.shape
    G = len(C_GROUPS)
    qkv = (h @ w_qkv).reshape(B, S, G, 3, C_HEADS, C_HEAD_DIM)
    q = apply_rope(qkv[:, :, :, 0], cos, sin) * (C_HEAD_DIM ** -0.5)
    k = apply_rope(qkv[:, :, :, 1], cos, sin)
    v = qkv[:, :, :, 2]
    outs, lses = [], []
    for g, (window, dilation) in enumerate(C_GROUPS):
        o_g, l_g = _dilated_group(q[:, :, g], k[:, :, g], v[:, :, g], window, dilation)
        outs.append(o_g)
        lses.append(l_g)
    wts = jax.nn.softmax(jnp.stack(lses, axis=0), axis=0)
    o = jnp.sum(wts[..., None].astype(v.dtype) * jnp.stack(outs, axis=0), axis=0)
    return o.reshape(B, S, C_HEADS * C_HEAD_DIM) @ w_o

def swiglu(h, w_gu, w_out):
    gu = h @ w_gu
    return (jax.nn.silu(gu[..., :FFN_DIM]) * gu[..., FFN_DIM:]) @ w_out

def _w(k, shape, fan_in):
    return jax.random.normal(k, shape, jnp.float32) * (fan_in ** -0.5)

def _gain(k, shape):
    return 1.0 + 0.02 * jax.random.normal(k, shape, jnp.float32)

def first_inputs(seed: int = 0) -> dict:
    key = jax.random.key(seed)
    ks = jax.random.split(key, 21)
    D = D_MODEL
    a_qkv = 2 * 2 * A_HEADS * A_HEAD_DIM + A_HEADS * A_V_DIM
    c_qkv = len(C_GROUPS) * 3 * C_HEADS * C_HEAD_DIM
    return {
        'x': jax.random.normal(ks[0], (BATCH, SEQ, D), jnp.float32),
        'attn_norm': _gain(ks[1], (DEPTH, D)),
        'ffn_norm': _gain(ks[2], (DEPTH, D)),
        'final_norm': _gain(ks[3], (D,)),
        'a_w_qkv': _w(ks[4], (N_A, D, a_qkv), D),
        'a_lambda_q1': 0.1 * jax.random.normal(ks[5], (N_A, A_HEAD_DIM), jnp.float32),
        'a_lambda_k1': 0.1 * jax.random.normal(ks[6], (N_A, A_HEAD_DIM), jnp.float32),
        'a_lambda_q2': 0.1 * jax.random.normal(ks[7], (N_A, A_HEAD_DIM), jnp.float32),
        'a_lambda_k2': 0.1 * jax.random.normal(ks[8], (N_A, A_HEAD_DIM), jnp.float32),
        'a_subln': _gain(ks[9], (N_A, A_V_DIM)),
        'a_w_o': _w(ks[10], (N_A, A_HEADS * A_V_DIM, D), A_HEADS * A_V_DIM),
        'b_w_a': _w(ks[11], (N_B, D, B_Q_RANK + B_KV_RANK + B_ROPE), D),
        'b_q_norm': _gain(ks[12], (N_B, B_Q_RANK)),
        'b_kv_norm': _gain(ks[13], (N_B, B_KV_RANK)),
        'b_w_qb': _w(ks[14], (N_B, B_Q_RANK, B_HEADS * (B_NOPE + B_ROPE)), B_Q_RANK),
        'b_w_kvb': _w(ks[15], (N_B, B_KV_RANK, B_HEADS * (B_NOPE + B_V)), B_KV_RANK),
        'b_w_o': _w(ks[16], (N_B, B_HEADS * B_V, D), B_HEADS * B_V),
        'c_w_qkv': _w(ks[17], (N_C, D, c_qkv), D),
        'c_w_o': _w(ks[18], (N_C, C_HEADS * C_HEAD_DIM, D), C_HEADS * C_HEAD_DIM),
        'f_w_gu': _w(ks[19], (DEPTH, D, 2 * FFN_DIM), D),
        'f_w_out': _w(ks[20], (DEPTH, FFN_DIM, D), FFN_DIM),
    }

def first_block(x, attn_norm, ffn_norm, final_norm, a_w_qkv, a_lambda_q1, a_lambda_k1, a_lambda_q2,
              a_lambda_k2, a_subln, a_w_o, b_w_a, b_q_norm, b_kv_norm, b_w_qb, b_w_kvb, b_w_o,
              c_w_qkv, c_w_o, f_w_gu, f_w_out):
    S = x.shape[1]
    cos_p, sin_p = rope_tables(S, A_ROT)
    cos_b, sin_b = rope_tables(S, B_ROPE)
    for i in range(DEPTH):
        m, j = i % N_MIXERS, i // N_MIXERS
        h = rms_norm(x, attn_norm[i])
        if m == 0:
            lambda_init = 0.8 - 0.6 * math.exp(-0.3 * i)
            mix = diff_attention(h, a_w_qkv[j], a_lambda_q1[j], a_lambda_k1[j], a_lambda_q2[j],
                                 a_lambda_k2[j], a_subln[j], a_w_o[j], lambda_init, cos_p, sin_p)
        elif m == 1:
            mix = latent_attention(h, b_w_a[j], b_q_norm[j], b_kv_norm[j], b_w_qb[j], b_w_kvb[j],
                                   b_w_o[j], cos_b, sin_b)
        else:
            mix = dilated_attention(h, c_w_qkv[j], c_w_o[j], cos_p, sin_p)
        x = x + mix
        x = x + swiglu(rms_norm(x, ffn_norm[i]), f_w_gu[i], f_w_out[i])
    return rms_norm(x, final_norm)


DEPTH_2 = 1

D_MIX = D_MODEL
D_SSM = D_MIX // 2
D_ATTN = D_MIX - D_SSM
SSM_GROUP = 16
N_SSM_GROUPS = D_SSM // SSM_GROUP
SSM_STATE = 64
DT_MIN = 1e-3
DT_MAX = 1e-1
HEAD_DIM = 64
N_HEADS = D_ATTN // HEAD_DIM
MOBA_BLOCK = 256
MOBA_TOPK = 3
Q_CHUNK = 16
D_FF = -(-8 * D_MODEL // (3 * 256)) * 256
RMS_EPS = 1e-6


def rmsnorm(x, g):
    xf = x.astype(jnp.float32)
    y = xf * lax.rsqrt(jnp.mean(xf * xf, axis=-1, keepdims=True) + RMS_EPS)
    return (y * g.astype(jnp.float32)).astype(x.dtype)

def _complex_affine_combine(e1, e2):
    a1r, a1i, b1r, b1i = e1
    a2r, a2i, b2r, b2i = e2
    ar = a2r * a1r - a2i * a1i
    ai = a2r * a1i + a2i * a1r
    br = a2r * b1r - a2i * b1i + b2r
    bi = a2r * b1i + a2i * b1r + b2i
    return (ar, ai, br, bi)

def s5_mixer(u, a_re, a_im, log_dt, b_re, b_im, c_re, c_im, d_skip, w_glu, b_glu):
    bsz, s, _ = u.shape
    f32 = jnp.float32
    uf = u.astype(f32).reshape(bsz, s, N_SSM_GROUPS, SSM_GROUP)
    a_re = a_re.astype(f32); a_im = a_im.astype(f32)
    dt = jnp.exp(log_dt.astype(f32))[:, None]
    mag = jnp.exp(a_re * dt)
    ang = a_im * dt
    lb_re = mag * jnp.cos(ang)
    lb_im = mag * jnp.sin(ang)
    nr = lb_re - 1.0
    den = a_re * a_re + a_im * a_im
    cr = (nr * a_re + lb_im * a_im) / den
    ci = (lb_im * a_re - nr * a_im) / den
    b_re = b_re.astype(f32); b_im = b_im.astype(f32)
    bb_re = cr[..., None] * b_re - ci[..., None] * b_im
    bb_im = cr[..., None] * b_im + ci[..., None] * b_re
    bu_re = jnp.einsum('bsgh,gph->bsgp', uf, bb_re)
    bu_im = jnp.einsum('bsgh,gph->bsgp', uf, bb_im)
    ar = jnp.broadcast_to(lb_re, (1, s) + lb_re.shape)
    ai = jnp.broadcast_to(lb_im, (1, s) + lb_im.shape)
    _, _, st_re, st_im = lax.associative_scan(
        _complex_affine_combine, (ar, ai, bu_re, bu_im), axis=1)
    y = (jnp.einsum('bsgp,ghp->bsgh', st_re, c_re.astype(f32))
         - jnp.einsum('bsgp,ghp->bsgh', st_im, c_im.astype(f32))
         + d_skip.astype(f32) * uf)
    y = jax.nn.gelu(y.reshape(bsz, s, D_SSM))
    y = y * jax.nn.sigmoid(jnp.einsum('bsc,ce->bse', y, w_glu.astype(f32)) + b_glu.astype(f32))
    return y.astype(u.dtype)

def moba_attention(q, k, v):
    bsz, s, _ = q.shape
    n_blocks = -(-s // MOBA_BLOCK)
    sp = n_blocks * MOBA_BLOCK
    k_sel = min(MOBA_TOPK, n_blocks)
    n_chunks = sp // Q_CHUNK

    def heads(t):
        t = t.astype(jnp.float32).reshape(bsz, s, N_HEADS, HEAD_DIM).transpose(0, 2, 1, 3)
        return jnp.pad(t, ((0, 0), (0, 0), (0, sp - s), (0, 0)))

    qh = heads(q) * (HEAD_DIM ** -0.5)
    kh = heads(k)
    vh = heads(v)
    k_blocks = kh.reshape(bsz, N_HEADS, n_blocks, MOBA_BLOCK, HEAD_DIM)
    v_blocks = vh.reshape(bsz, N_HEADS, n_blocks, MOBA_BLOCK, HEAD_DIM)
    k_mean = jnp.mean(k_blocks, axis=3)

    gate = jnp.einsum('bhsd,bhnd->bhsn', qh, k_mean)
    q_blk = jnp.arange(sp) // MOBA_BLOCK
    past = jnp.arange(n_blocks)[None, :] < q_blk[:, None]
    gate = jnp.where(past, gate, -jnp.inf)
    _, sel_idx = lax.top_k(gate, k_sel)
    sel_valid = jnp.arange(k_sel)[None, :] < q_blk[:, None]

    def to_chunks(t):
        return jnp.moveaxis(t.reshape(bsz, N_HEADS, n_chunks, Q_CHUNK, *t.shape[3:]), 2, 0)

    q_c = to_chunks(qh)
    idx_c = to_chunks(sel_idx)
    valid_c = sel_valid.reshape(n_chunks, Q_CHUNK, k_sel)
    gather = jax.vmap(jax.vmap(lambda blocks, ix: blocks[ix]))

    def chunk_attend(args):
        c, qc, ic, vc = args
        kg = gather(k_blocks, ic)
        vg = gather(v_blocks, ic)
        s_sel = jnp.einsum('bhqd,bhqnjd->bhqnj', qc, kg)
        s_sel = jnp.where(vc[None, None, :, :, None], s_sel, -jnp.inf)
        own = (c * Q_CHUNK) // MOBA_BLOCK
        k_own = lax.dynamic_index_in_dim(k_blocks, own, axis=2, keepdims=False)
        v_own = lax.dynamic_index_in_dim(v_blocks, own, axis=2, keepdims=False)
        s_own = jnp.einsum('bhqd,bhjd->bhqj', qc, k_own)
        q_pos = c * Q_CHUNK + jnp.arange(Q_CHUNK)
        k_pos = own * MOBA_BLOCK + jnp.arange(MOBA_BLOCK)
        s_own = jnp.where(k_pos[None, :] <= q_pos[:, None], s_own, -jnp.inf)
        scores = jnp.concatenate(
            [s_sel.reshape(bsz, N_HEADS, Q_CHUNK, k_sel * MOBA_BLOCK), s_own], axis=-1)
        p = jax.nn.softmax(scores, axis=-1)
        p_sel = p[..., :k_sel * MOBA_BLOCK].reshape(bsz, N_HEADS, Q_CHUNK, k_sel, MOBA_BLOCK)
        p_own = p[..., k_sel * MOBA_BLOCK:]
        return (jnp.einsum('bhqnj,bhqnjd->bhqd', p_sel, vg)
                + jnp.einsum('bhqj,bhjd->bhqd', p_own, v_own))

    out = lax.map(chunk_attend, (jnp.arange(n_chunks), q_c, idx_c, valid_c))
    out = out.transpose(1, 0, 3, 2, 4).reshape(bsz, sp, D_ATTN)
    return out[:, :s].astype(q.dtype)

def hybrid_layer(x, g_pre_mix, w_in, ssm_a_re, ssm_a_im, ssm_log_dt, ssm_b_re, ssm_b_im,
                 ssm_c_re, ssm_c_im, ssm_d, w_glu, b_glu, g_ssm_out, g_attn_out, w_out,
                 g_post_mix, g_pre_ffn, w_gate, w_up, w_down, g_post_ffn):
    h = rmsnorm(x, g_pre_mix)
    z = jnp.einsum('bsd,de->bse', h, w_in)
    u, q, k, v = jnp.split(z, [D_SSM, D_SSM + D_ATTN, D_SSM + 2 * D_ATTN], axis=-1)
    y_ssm = s5_mixer(u, ssm_a_re, ssm_a_im, ssm_log_dt, ssm_b_re, ssm_b_im,
                     ssm_c_re, ssm_c_im, ssm_d, w_glu, b_glu)
    y_attn = moba_attention(q, k, v)
    mix = jnp.concatenate([rmsnorm(y_ssm, g_ssm_out), rmsnorm(y_attn, g_attn_out)], axis=-1)
    x = x + rmsnorm(jnp.einsum('bse,ed->bsd', mix, w_out), g_post_mix)
    h = rmsnorm(x, g_pre_ffn)
    f = jax.nn.silu(jnp.einsum('bsd,df->bsf', h, w_gate)) * jnp.einsum('bsd,df->bsf', h, w_up)
    x = x + rmsnorm(jnp.einsum('bsf,fd->bsd', f, w_down), g_post_ffn)
    return x

def second_inputs(seed: int = 0) -> dict:
    key = jax.random.key(seed)
    ks = jax.random.split(key, 24)
    f32 = jnp.float32
    G, P, H = N_SSM_GROUPS, SSM_STATE, SSM_GROUP
    L = DEPTH_2

    def nrm(k, shape, scale):
        return jax.random.normal(k, shape, f32) * scale

    def gain(k, n):
        return 1.0 + 0.01 * jax.random.normal(k, (L, n), f32)

    n_idx = jnp.arange(P, dtype=f32)
    return dict(
        x=nrm(ks[0], (BATCH, SEQ, D_MODEL), 1.0),
        g_pre_mix=gain(ks[1], D_MODEL),
        w_in=nrm(ks[2], (L, D_MODEL, D_SSM + 3 * D_ATTN), D_MODEL ** -0.5),
        ssm_a_re=-0.5 + nrm(ks[3], (L, G, P), 0.01),
        ssm_a_im=math.pi * n_idx[None, None, :] + nrm(ks[4], (L, G, P), 0.01),
        ssm_log_dt=jax.random.uniform(ks[5], (L, G), f32, minval=math.log(DT_MIN), maxval=math.log(DT_MAX)),
        ssm_b_re=nrm(ks[6], (L, G, P, H), (2 * H) ** -0.5),
        ssm_b_im=nrm(ks[7], (L, G, P, H), (2 * H) ** -0.5),
        ssm_c_re=nrm(ks[8], (L, G, H, P), (2 * P) ** -0.5),
        ssm_c_im=nrm(ks[9], (L, G, H, P), (2 * P) ** -0.5),
        ssm_d=nrm(ks[10], (L, G, H), 1.0),
        w_glu=nrm(ks[11], (L, D_SSM, D_SSM), D_SSM ** -0.5),
        b_glu=nrm(ks[12], (L, D_SSM), 0.01),
        g_ssm_out=gain(ks[13], D_SSM),
        g_attn_out=gain(ks[14], D_ATTN),
        w_out=nrm(ks[15], (L, D_MIX, D_MODEL), D_MIX ** -0.5),
        g_post_mix=gain(ks[16], D_MODEL),
        g_pre_ffn=gain(ks[17], D_MODEL),
        w_gate=nrm(ks[18], (L, D_MODEL, D_FF), D_MODEL ** -0.5),
        w_up=nrm(ks[19], (L, D_MODEL, D_FF), D_MODEL ** -0.5),
        w_down=nrm(ks[20], (L, D_FF, D_MODEL), D_FF ** -0.5),
        g_post_ffn=gain(ks[21], D_MODEL),
    )

def second_block(x, g_pre_mix, w_in, ssm_a_re, ssm_a_im, ssm_log_dt, ssm_b_re, ssm_b_im,
              ssm_c_re, ssm_c_im, ssm_d, w_glu, b_glu, g_ssm_out, g_attn_out, w_out,
              g_post_mix, g_pre_ffn, w_gate, w_up, w_down, g_post_ffn):
    for l in range(DEPTH_2):
        x = hybrid_layer(x, g_pre_mix[l], w_in[l], ssm_a_re[l], ssm_a_im[l], ssm_log_dt[l],
                         ssm_b_re[l], ssm_b_im[l], ssm_c_re[l], ssm_c_im[l], ssm_d[l],
                         w_glu[l], b_glu[l], g_ssm_out[l], g_attn_out[l], w_out[l],
                         g_post_mix[l], g_pre_ffn[l], w_gate[l], w_up[l], w_down[l], g_post_ffn[l])
    return x


_first_inputs = second_inputs


def second_inputs(seed=0):
    import zlib

    import numpy as np

    out = dict(_first_inputs(seed))
    spreads = {}
    factors = {'g_pre_mix': 4.4,
     'ssm_a_re': 64.0,
     'b_glu': 27.917,
     'g_ssm_out': 54.538,
     'g_attn_out': 54.665,
     'g_post_mix': 32.269,
     'g_pre_ffn': 37.171,
     'g_post_ffn': 58.642,
     'ssm_b_re': 3.03,
     'ssm_b_im': 3.014,
     'ssm_c_re': 3.039,
     'ssm_c_im': 3.015}
    for name, (base, spread) in spreads.items():
        noise = np.random.default_rng([zlib.crc32(name.encode()), seed]).standard_normal(out[name].shape)
        drawn = base * np.exp(spread * noise) if base else spread * noise
        out[name] = __import__('jax').numpy.asarray(drawn.astype(out[name].dtype))
    for name, factor in factors.items():
        out[name] = (out[name] * factor).astype(out[name].dtype)
    return out


_narrow_inputs = second_inputs


def second_inputs(seed=0):

    out = dict(_narrow_inputs(seed))
    wider = {'ssm_a_re': 12.0,
     'g_ssm_out': 7.17,
     'g_attn_out': 7.18,
     'g_post_mix': 4.86,
     'g_pre_ffn': 5.24,
     'g_post_ffn': 7.06}
    for name, times in wider.items():
        mean = out[name].mean()
        out[name] = (mean + times * (out[name] - mean)).astype(out[name].dtype)
    return out


def setup_inputs(seed=0):
    out = dict(first_inputs(seed))
    for name, value in second_inputs(seed + 1).items():
        if name != "x":
            out[name + "_2"] = value
    return out


def reference(
    x, attn_norm, ffn_norm, final_norm, a_w_qkv, a_lambda_q1, a_lambda_k1, a_lambda_q2,
    a_lambda_k2, a_subln, a_w_o, b_w_a, b_q_norm, b_kv_norm, b_w_qb, b_w_kvb, b_w_o, c_w_qkv,
    c_w_o, f_w_gu, f_w_out, g_pre_mix_2, w_in_2, ssm_a_re_2, ssm_a_im_2, ssm_log_dt_2,
    ssm_b_re_2, ssm_b_im_2, ssm_c_re_2, ssm_c_im_2, ssm_d_2, w_glu_2, b_glu_2, g_ssm_out_2,
    g_attn_out_2, w_out_2, g_post_mix_2, g_pre_ffn_2, w_gate_2, w_up_2, w_down_2, g_post_ffn_2,
):
    x = first_block(
        x, attn_norm, ffn_norm, final_norm, a_w_qkv, a_lambda_q1, a_lambda_k1, a_lambda_q2,
        a_lambda_k2, a_subln, a_w_o, b_w_a, b_q_norm, b_kv_norm, b_w_qb, b_w_kvb, b_w_o,
        c_w_qkv, c_w_o, f_w_gu, f_w_out,
    )
    return second_block(
        x, g_pre_mix_2, w_in_2, ssm_a_re_2, ssm_a_im_2, ssm_log_dt_2, ssm_b_re_2, ssm_b_im_2,
        ssm_c_re_2, ssm_c_im_2, ssm_d_2, w_glu_2, b_glu_2, g_ssm_out_2, g_attn_out_2, w_out_2,
        g_post_mix_2, g_pre_ffn_2, w_gate_2, w_up_2, w_down_2, g_post_ffn_2,
    )


_drawn_inputs = setup_inputs


def setup_inputs(seed=0):
    import zlib

    import numpy as np

    out = dict(_drawn_inputs(seed))
    spreads = {}
    factors = {'b_q_norm': 6.503}
    for name, (base, spread) in spreads.items():
        noise = np.random.default_rng([zlib.crc32(name.encode()), seed]).standard_normal(out[name].shape)
        drawn = base * np.exp(spread * noise) if base else spread * noise
        out[name] = jnp.asarray(drawn.astype(out[name].dtype))
    for name, factor in factors.items():
        out[name] = (out[name] * factor).astype(out[name].dtype)
    return out
```

```python
from contextlib import ExitStack

import numpy as np

import concourse.bass as bass
from concourse import mybir

F32 = mybir.dt.float32
F32R = mybir.dt.float32r
I32 = mybir.dt.int32
ALU = mybir.AluOpType
ACT = mybir.ActivationFunctionType
AX_X = mybir.AxisListType.X

P = 128
S = 256
T2 = S // P
D = 1024
KD = D // P
BANK = 512
FFN = 2816
CHUNKS = FFN // P
EPS = 1e-6
TILE = 2048
RING = 3
LEAD = 2
SPLIT_DVE = 1024
LOWEST = -3.0e38
MAGIC = 12582912.0
TURN = 6.283185307179586
TURN_HI = 6.28125
TURN_LO = TURN - TURN_HI


class Place:

    def __init__(self, base, turns=0):
        self.base, self.turns = base, turns

    def __add__(self, n):
        return Place(self.base + n, self.turns)

    @property
    def slot(self):
        return self.base % RING

    @property
    def count(self):
        return self.turns * RING + self.base

    @property
    def round(self):
        return self.turns + self.base // RING


LAYERS = (0, 1, 2, 3)


def lambda_init(layer):
    return 0.8 - 0.6 * float(np.exp(-0.3 * layer))


class Stage:

    def __init__(self, kind, at, src="xs", kts=KD, gain=None, groups=1, mix=None, j=0, post=None):
        self.kind, self.src, self.kts, self.gain = kind, src, kts, gain
        self.groups, self.mix, self.j, self.post = groups, mix, j, post
        self.tile, self.slab, self.rope, self.turned = at["tile"], at["slab"], at["rope"], at["turned"]
        self.unit, self.mixes, self.pta, self.ptd = at["unit"], at["mixes"], at["pta"], at["ptd"]
        self.obank, self.operand, self.chunk, self.pair = at["obank"], at["operand"], at["chunk"], at["pair"]
        self.norms, self.xsd, self.x_ready, self.rows = at["norms"], at["xsd"], at["x_ready"], at["rows"]


def plan():
    stages = []
    c = dict(tile=0, slab=0, rope=0, turned=0, unit=0, mixes=0, pta=0, ptd=0, obank=0, operand=0, chunk=0, pair=0, norms=0, xsd=0, x_ready=0, rows=0)

    def add(kind, uses, **k):
        stages.append(Stage(kind, c, **k))
        for n, v in uses.items():
            c[n] += v

    for layer in LAYERS:
        if layer == LAYERS[-1]:
            add("fetch", dict())
        mixer = ("A", "B", "C")[layer % 3]
        add("norm", dict(norms=1, xsd=1), gain=f"attn_norm{layer}")
        add("operand", dict(operand=4), src="xs", kts=KD, gain=f"attn_norm{layer}")
        if mixer == "A":
            add("qkv", dict(tile=12, slab=6, rope=4, turned=4), groups=1)
            add("attend", dict(unit=16, mixes=16, pta=16, obank=4, xsd=1), mix="A", j=layer // 3)
            add("operand", dict(operand=4), src="xs", kts=KD, gain=f"subln{layer // 3}")
            add("out", dict(tile=4, x_ready=1), post=None)
        elif mixer == "B":
            add("latent", dict(tile=3, slab=2))
            add("operand", dict(operand=3), src="lat", kts=5, gain="lat")
            add("lift", dict(tile=5, slab=7, turned=8))
            add("attend", dict(unit=32, ptd=32, obank=4), mix="B")
            add("operand", dict(operand=4), src="xs", kts=KD, gain=None)
            add("out", dict(tile=4, x_ready=1), post=None)
        else:
            add("qkv", dict(tile=36, slab=18, rope=12, turned=12), groups=3)
            add("attend", dict(unit=32, pta=32, ptd=32, obank=4), mix="C")
            add("operand", dict(operand=4), src="xs", kts=KD, gain=None)
            add("out", dict(tile=4, x_ready=1), post=None)
        add("norm", dict(norms=1, xsd=1), gain=f"ffn_norm{layer}")
        add("operand", dict(operand=4), src="xs", kts=KD, gain=f"ffn_norm{layer}")
        add("ffn", dict(tile=33, chunk=22, pair=11, x_ready=1), post=None)
    add("final_norm", dict(x_ready=1, rows=1))
    add("norm", dict(norms=1, xsd=1), gain="pre_mix")
    add("operand", dict(operand=4), src="xs", kts=KD, gain="pre_mix")
    add("hybrid", dict(tile=9, slab=4, turned=3, unit=16, ptd=16, obank=2, operand=2), mix="M")
    add("out", dict(tile=4, x_ready=1, rows=1), post="post_mix")
    add("norm", dict(norms=1, xsd=1), gain="pre_ffn")
    add("operand", dict(operand=4), src="xs", kts=KD, gain="pre_ffn")
    add("ffn", dict(tile=33, chunk=22, pair=11, x_ready=1, rows=1), post="post_ffn")
    return stages, c["tile"]



SMALL = {}


def _small(name, width):
    SMALL[name] = (sum(w for _, w in SMALL.values()), width)


for _l in range(4):
    _small(f"attn_norm{_l}", KD)
    _small(f"ffn_norm{_l}", KD)
_small("lat", 5)
_small("subln0", 1)
_small("subln1", 1)
_small("pre_mix", KD)
_small("pre_ffn", KD)
_small("ssm_out", 4)
_small("attn_out", 4)
_small("b_glu", 4)
_small("ssm_d", 4)
_small("a_re", 16)
_small("a_im", 16)
_small("log_dt", 16)
SMALL_W = sum(w for _, w in SMALL.values())
CONST = {}


def _const(name, width):
    CONST[name] = (sum(w for _, w in CONST.values()), width)


_const("ident", P)
_const("cos_a", T2 * 16)
_const("sin_a", T2 * 16)
_const("cos_b", T2 * 32)
_const("sin_b", T2 * 32)
_const("mask", 1024)
_const("causal", 384)
_const("ones", P)
CONST_W = sum(w for _, w in CONST.values())


STATES = 64
GROUPS = 32
GIN = 16
STILES = GROUPS * STATES // P
SHIFTS = 8
S5_W = 2 * 4 * P + 2 * STILES * 32


def build_program(nc, x_in, tape, smalls, consts, lam_in, rows_in, s5_in, out):
    stages, tiles = plan()
    hybrid = next(st for st in stages if st.kind == "hybrid")
    with ExitStack() as ctx:
        def sem(name):
            return ctx.enter_context(nc.semaphore(name))

        def psum(name, shape):
            return ctx.enter_context(nc.psum_tensor(name, shape, F32))

        place = {"at": 0}
        room = ctx.enter_context(nc.sbuf_tensor("room", [P, (nc.sbuf_bytes_remaining - 64) // 4], F32))
        base = nc.sbuf_base - room.shape[1] * 4

        def sb(name, shape, dt=F32, at=None):
            size = 4 * int(np.prod(shape[1:]))
            if at is None:
                at = place["at"]
                place["at"] += -(-size // 32) * 32
                assert place["at"] <= room.shape[1] * 4, (name, place["at"])
            return nc.alloc_sbuf_tensor_at(name, shape, dt, offset=base + at)

        raw = sb("raw", [P, RING, TILE])
        w_hi = sb("w_hi", [P, RING, TILE], F32R)
        w_lo = sb("w_lo", [P, RING, TILE], F32R)
        x = sb("x", [P, T2, D])
        xs = sb("xs", [P, T2, D])
        xT_hi = sb("xT_hi", [P, KD, S], F32R)
        xT_lo = sb("xT_lo", [P, KD, S], F32R)
        small = sb("small", [P, SMALL_W])
        const = sb("const", [P, CONST_W])
        stat = sb("stat", [P, 5, 16])
        sums = sb("sums", [P, 2, 32])
        nmax = sb("nmax", [P, 2, 2])
        lam = sb("lam", [P, 16])
        rot = sb("rot", [P, 2, 256])
        scratch_at = place["at"]
        probs = sb("probs", [P, 2, 768])
        probsT = sb("probsT", [P, 2, 6, P])
        hT_hi = sb("hT_hi", [P, 2, 2, S], F32R, at=scratch_at)
        hT_lo = sb("hT_lo", [P, 2, 2, S], F32R, at=scratch_at + 2 * 2 * S * 4)
        stage = sb("stage", [P, 2, T2, BANK], at=scratch_at)
        arena_at = place["at"]
        QT = sb("QT", [P, 24, S])
        KT = sb("KT", [P, 24, S])
        V = sb("V", [P, 3, T2, D])
        squared = sb("squared", [P, 16, P], at=arena_at + 8192)
        h32 = sb("h32", [P, 2, 2, S], at=arena_at)
        sg = sb("sg", [P, 2, S], at=arena_at + 4096)
        q_tm = sb("q_tm", [P, T2, 1536], at=arena_at)
        k_tm = sb("k_tm", [P, T2, 1536], at=arena_at + 12288)
        QB = sb("QB", [96, 16, S], at=arena_at + 24576)
        KB = sb("KB", [96, 16, S], at=arena_at + 40960)
        a_tm = sb("a_tm", [P, T2, 672], at=arena_at + 57344)
        V_B = sb("V_B", [P, T2, D], at=arena_at + 63488)
        y_skip = sb("y_skip", [P, 4, S], at=arena_at + 4096)
        E_re = sb("E_re", [P, STILES, S], at=arena_at + 8192)
        E_im = sb("E_im", [P, STILES, S], at=arena_at + 28672)
        row = sb("row", [P, D], at=arena_at + 45056)
        s5 = sb("s5", [P, S5_W], at=arena_at + 57344)
        Cc = sb("Cc", [P, 2, STILES, 32], at=arena_at + 57344 + 4 * S5_W)
        uT = sb("uT", [P, 4, S], at=arena_at + 57344 + 4 * S5_W + 4096)
        B_in = s5[:, 0:1024].rearrange("p (c f n) -> p c f n", c=2, f=4)
        C_in = s5[:, 1024:2048].rearrange("p (c i n) -> p c i n", c=2, i=STILES)
        xT_at = (RING * TILE * 3 + 2 * T2 * D) * 4
        pre_c = sb("pre_c", [P, 2, S], at=xT_at)
        pre_s = sb("pre_s", [P, 2, S], at=xT_at + 2048)
        scan = sb("scan", [P, 2, 2, S], at=xT_at + 4096)
        post_c = sb("post_c", [P, 2, 2, S], at=xT_at + 8192)
        post_s = sb("post_s", [P, 2, S], at=xT_at + 12288)
        y_act = sb("y_act", [P, 4, S], at=arena_at + 8192)
        sig = sb("sig", [P, 4, S], at=arena_at + 12288)
        y_gated = sb("y_gated", [P, 4, S], at=arena_at + 16384)
        y_sq = sb("y_sq", [P, 4, S], at=arena_at + 20480)
        inv3 = sb("inv3", [P, 3, S], at=arena_at + 28672)
        y_norm = sb("y_norm", [P, 4, S], at=arena_at + 32768)
        q_tmp = sb("q_tmp", [P, 2, 512], at=arena_at + 4096)
        h_junk = sb("h_junk", [P, T2, D], at=arena_at + 8192)
        pole = sb("pole", [P, 12, STILES], at=scratch_at + 10240)
        trig = sb("trig", [P, 2, SHIFTS, STILES], at=scratch_at + 11008)
        trig_k = sb("trig_k", [P, 2, SHIFTS, STILES], at=scratch_at + 8192)

        bank = psum("bank", [P, 8, BANK])
        ident = const[:, 0:P]

        def const_ap(name):
            o, w = CONST[name]
            return const[:, o:o + w]

        def gain(name, k):
            return small[:, SMALL[name][0] + k:SMALL[name][0] + k + 1]

        def gains(name):
            o, w = SMALL[name]
            return small[:, o:o + w]

        small_in = sem("small_in")
        x_in_done = sem("x_in_done")
        tape_in = [sem(f"tape_in{i}") for i in range(RING)]
        hi_done = sem("hi_done")
        lo_dve = sem("lo_dve")
        lo_pool = sem("lo_pool")
        w_used = sem("w_used")
        chain = sem("chain")
        inv_ready = sem("inv_ready")
        xs_dve = sem("xs_dve")
        xs_act = sem("xs_act")
        op_turned = sem("op_turned")
        op_hi = sem("op_hi")
        op_lo = sem("op_lo")
        slab_out = sem("slab_out")
        rope_mul = sem("rope_mul")
        rope_done = sem("rope_done")
        turned = sem("turned")
        turned_out = sem("turned_out")
        scores = sem("scores")
        maxed = sem("maxed")
        exped = sem("exped")
        mixed = sem("mixed")
        probs_turned = sem("probs_turned")
        pt_act = sem("pt_act")
        pt_dve = sem("pt_dve")
        o_done = sem("o_done")
        o_out = sem("o_out")
        o_sq = sem("o_sq")
        gu_done = sem("gu_done")
        silu_done = sem("silu_done")
        h_done = sem("h_done")
        h_hi = sem("h_hi")
        h_lo = sem("h_lo")
        lam_dots = sem("lam_dots")
        lam_exp = sem("lam_exp")
        sq_act = sem("sq_act")
        x_ready = sem("x_ready")
        lat_ready = sem("lat_ready")
        out_ready = sem("out_ready")
        stored = sem("stored")
        s5_in_done = sem("s5_in_done")
        row_in = sem("row_in")
        row_used = sem("row_used")
        dt_ready = sem("dt_ready")
        pole_ready = sem("pole_ready")
        mag_ready = sem("mag_ready")
        angle_ready = sem("angle_ready")
        trig_ready = sem("trig_ready")
        v_done = sem("v_done")
        v_used = sem("v_used")
        scanned = sem("scanned")
        states = sem("states")
        pool_chain = sem("pool_chain")
        y_done = sem("y_done")
        y_out = sem("y_out")
        gelu_done = sem("gelu_done")
        glu_hi = sem("glu_hi")
        glu_lo = sem("glu_lo")
        sig_done = sem("sig_done")
        sq_done = sem("sq_done")
        ss_done = sem("ss_done")
        norm_done = sem("norm_done")
        mix_hi = sem("mix_hi")
        mix_lo = sem("mix_lo")
        hybrid_xs = sem("hybrid_xs")

        block = ctx.enter_context(nc.Block())

        def lo_part(eng, at, lo, hi):
            eng.wait_ge(hi_done, at.count + 1)
            return eng.tensor_tensor(w_lo[:, at.slot, lo:hi], raw[:, at.slot, lo:hi],
                                     w_hi[:, at.slot, lo:hi].bitcast(F32), ALU.subtract)

        def unit_list(st):
            heads = {"A": 8, "B": 16, "C": 16, "M": 8}[st.mix]
            return [(h, t) for h in range(heads) for t in range(T2)]

        def turn_banks(st, u):
            return (4, 5) if st.mix == "C" else (4,) if st.mix == "M" else (4 + u % 2,)

        def group_order(st, t):
            if st.mix == "C":
                return (0, 1, 2) if t == 0 else (1, 2, 0)
            return (0,)

        @block.sync
        def _(sp):
            sp.dma_start(x[:], x_in.rearrange("(t p) d -> p t d", p=P)).then_inc(x_in_done, 16)
            for n in range(RING):
                sp.dma_start(raw[:, n, :], tape[n]).then_inc(tape_in[n], 16)
            sp.dma_start(small[:], smalls).then_inc(small_in, 16)
            sp.dma_start(const[:], consts).then_inc(small_in, 16)
            sp.dma_start(V[:, 0, 0, 0:512], lam_in.partition_broadcast(P)).then_inc(small_in, 16)

            def load(at):
                sp.wait_ge(lo_dve, at.count - RING + 1)
                sp.wait_ge(lo_pool, at.count - RING + 1)
                sp.dma_start(raw[:, at.slot, :], tape[bass.ds(at.count, 1), :, :].rearrange("a p n -> (a p) n")
                             ).then_inc(tape_in[at.slot], 16)

            turns = tiles // RING
            with sp.Fori(1, turns) as turn:
                for slot in range(RING):
                    load(Place(slot, turn))
            for n in range(turns * RING, tiles):
                load(Place(n))
            sp.wait_ge(out_ready, 1)
            sp.dma_start(out.rearrange("(t p) d -> p t d", p=P), x[:]).then_inc(stored, 16)
            sp.wait_ge(stored, 16)

        @block.gpsimd
        def _(pool):
            def low_parts(first, end):
                a = min(-(-first // RING) * RING, end)
                b = max(end // RING * RING, a)
                for n in range(first, a):
                    lo_part(pool, Place(n), SPLIT_DVE, TILE).then_inc(lo_pool, 1)
                if b > a:
                    with pool.Fori(a // RING, b // RING) as turn:
                        for slot in range(RING):
                            lo_part(pool, Place(slot, turn), SPLIT_DVE, TILE).then_inc(lo_pool, 1)
                for n in range(b, end):
                    lo_part(pool, Place(n), SPLIT_DVE, TILE).then_inc(lo_pool, 1)

            def link(ins, links):
                links[0] += 1
                ins.then_inc(pool_chain, 1)
                pool.wait_ge(pool_chain, links[0])

            def rotate_back(links):
                for i in range(STILES):
                    er = E_re[:, i, :].unsqueeze(1).broadcast_to([P, 2, S])
                    ei = E_im[:, i, :].unsqueeze(1).broadcast_to([P, 2, S])
                    pc = post_c[:, i % 2, :, :]
                    pool.wait_ge(scanned, i + 1)
                    if i >= 2:
                        pool.wait_ge(y_done, i - 1)
                    if i >= 1:
                        pool.wait_ge(states, i)
                    pool.tensor_tensor(pc, scan[:, i % 2, :, :], er, ALU.mult)
                    link(pool.tensor_tensor(post_s[:, :, :], scan[:, i % 2, :, :], ei, ALU.mult), links)
                    pool.tensor_tensor(pc[:, 0, :], pc[:, 0, :], post_s[:, 1, :], ALU.subtract)
                    pool.tensor_tensor(pc[:, 1, :], pc[:, 1, :], post_s[:, 0, :], ALU.add).then_inc(states, 1)

            stop = hybrid.tile + 8 + LEAD
            low_parts(0, stop)
            rotate_back([0])
            low_parts(stop, tiles)

        @block.tensor
        def _(pe):
            def weights(at):
                pe.wait_ge(lo_dve, at.count + 1)
                pe.wait_ge(lo_pool, at.count + 1)

            def product(o, l_hi, l_lo, r_hi, r_lo, start, stop):
                pe.matmul(o, l_hi, r_hi, start=start, stop=False)
                pe.matmul(o, l_hi, r_lo, start=False, stop=False)
                return pe.matmul(o, l_lo, r_hi, start=False, stop=stop)

            def operand_ready(st):
                pe.wait_ge(op_lo, st.operand)

            def operand(st):
                if st.src == "xs":
                    pe.wait_ge(xs_dve, st.xsd)
                    pe.wait_ge(xs_act, st.norms)
                    if st.obank:
                        pe.wait_ge(o_out, st.obank)
                else:
                    pe.wait_ge(lat_ready, 1)
                if st.operand == 0:
                    pe.wait_ge(small_in, 48)
                for b in range(-(-st.kts // 2)):
                    ks = range(2 * b, min(2 * b + 2, st.kts))
                    for k in ks:
                        for t in range(T2):
                            src = (xs if st.src == "xs" else a_tm)[:, t, k * P:(k + 1) * P]
                            o = (k % 2) * S + t * P
                            last = pe.transpose(bank[:, 4 + b, o:o + P], src, ident)
                    last.then_inc(op_turned, 1)

            def qkv_slab(at, s_count, pair, check):
                if check:
                    pe.wait_ge(slab_out, s_count - 1)
                for half in range(2):
                    weights(at + half)
                    for kk in range(4):
                        k = half * 4 + kk
                        for t in range(T2):
                            sl = (at + half).slot
                            last = product(bank[:, 2 * pair + t, :],
                                           xT_hi[:, k, t * P:(t + 1) * P], xT_lo[:, k, t * P:(t + 1) * P],
                                           w_hi[:, sl, kk * BANK:(kk + 1) * BANK],
                                           w_lo[:, sl, kk * BANK:(kk + 1) * BANK],
                                           start=(k == 0), stop=(k == KD - 1))
                    last.then_inc(w_used, 1)

            def turn_stage(s, rope_count, turned_count, buf, pair, check):
                pe.wait_ge(rope_done, rope_count + 1)
                if check:
                    pe.wait_ge(turned_out, turned_count - 1)
                for ft in range(4):
                    for t in range(T2):
                        b, o = divmod(ft * S + t * P, BANK)
                        last = pe.transpose(bank[:, 4 + 2 * pair + b, o:o + P],
                                            stage[:, buf, t, ft * P:(ft + 1) * P], ident)
                last.then_inc(turned, 1)

            def qkv_group(at, s0, r0, t0, check):
                for s in range(6):
                    qkv_slab(at + 2 * s, s0 + s, s % 2, check or s >= 2)
                    if 1 <= s <= 4:
                        turn_stage(s - 1, r0 + s - 1, t0 + s - 1, (s - 1) % 2, (s - 1) % 2, check or s >= 3)

            def qkv(st):
                operand_ready(st)
                if st.groups == 1:
                    qkv_group(Place(st.tile), st.slab, st.rope, st.turned, st.slab >= 2)
                else:
                    with pe.Fori(0, st.groups) as g:
                        qkv_group(Place(st.tile, g * 4), g * 6 + st.slab, g * 4 + st.rope,
                                  g * 4 + st.turned, True)

            def latent(st):
                operand_ready(st)
                qkv_slab(Place(st.tile), st.slab, 0, True)
                at = Place(st.tile + 2)
                pe.wait_ge(slab_out, st.slab)
                weights(at)
                for t in range(T2):
                    for k in range(KD):
                        last = product(bank[:, 2 + t, 0:160], xT_hi[:, k, t * P:(t + 1) * P],
                                       xT_lo[:, k, t * P:(t + 1) * P], w_hi[:, at.slot, k * 160:(k + 1) * 160],
                                       w_lo[:, at.slot, k * 160:(k + 1) * 160], start=(k == 0), stop=(k == KD - 1))
                last.then_inc(w_used, 1)

            def lift(st):
                operand_ready(st)
                s = st.slab
                for i in range(7):
                    at, lo, kts, k0 = (Place(st.tile + i), 0, 3, 0) if i < 3 else \
                        (Place(st.tile + 3 + (i - 3) // 2), ((i - 3) % 2) * BANK, 2, 3)
                    width = BANK if i < 3 else 2 * BANK
                    pe.wait_ge(slab_out, s + i - 1)
                    weights(at)
                    for k in range(kts):
                        for t in range(T2):
                            c = k * width + lo
                            last = product(bank[:, 2 * (i % 2) + t, :], xT_hi[:, k0 + k, t * P:(t + 1) * P],
                                           xT_lo[:, k0 + k, t * P:(t + 1) * P], w_hi[:, at.slot, c:c + BANK],
                                           w_lo[:, at.slot, c:c + BANK], start=(k == 0), stop=(k == kts - 1))
                    if i < 3 or i % 2 == 0:
                        last.then_inc(w_used, 1)
                for i in range(8):
                    if i == 0:
                        pe.wait_ge(lat_ready, 2)
                    if i == 4:
                        pe.wait_ge(lat_ready, 3)
                        pe.wait_ge(slab_out, s + 7)
                    pe.wait_ge(turned_out, st.turned + i - 1)
                    src = q_tm if i < 4 else k_tm
                    for hh in range(4):
                        for t in range(T2):
                            h = (i % 4) * 4 + hh
                            b, o = divmod(hh * S + t * P, BANK)
                            last = pe.transpose(bank[0:96, 4 + 2 * (i % 2) + b, o:o + P],
                                                src[:, t, h * 96:(h + 1) * 96], ident)
                    last.then_inc(turned, 1)

            def attend(st, beside=lambda u: None):
                units = unit_list(st)
                U = st.unit
                pe.wait_ge(turned_out, st.turned + (3 if st.mix == "M" else 0))
                pe.wait_ge(slab_out, st.slab + (4 if st.mix == "M" else 0))

                def score(u):
                    h, t = units[u]
                    if u >= 2:
                        pe.wait_ge(maxed if st.mix in "CM" else exped, U + u - 1)
                    b = 2 * (u % 2)
                    if st.mix == "A":
                        for sub in range(2):
                            p0 = sub * 64
                            last = pe.matmul(bank[:, b + sub, 0:S],
                                             QT[p0:p0 + 64, h, t * P:(t + 1) * P], KT[p0:p0 + 64, h, :],
                                             start=True, stop=True)
                    elif st.mix == "B":
                        last = pe.matmul(bank[:, b, 0:S], QB[:, h, t * P:(t + 1) * P], KB[:, h, :],
                                         start=True, stop=True)
                    else:
                        p0 = (h % 2) * 64
                        order = group_order(st, t)
                        for i, g in enumerate(order):
                            f = g * 8 + h // 2
                            bb, o = divmod(i * S, BANK)
                            last = pe.matmul(bank[:, b + bb, o:o + S], QT[p0:p0 + 64, f, t * P:(t + 1) * P],
                                             KT[p0:p0 + 64, f, :], start=True, stop=True)
                    last.then_inc(scores, 1)

                def transposed(u):
                    if st.mix in "AC":
                        pe.wait_ge(pt_act, st.pta + u + 1)
                    if st.mix in "BCM":
                        pe.wait_ge(pt_dve, st.ptd + u + 1)

                def turn(u):
                    pe.wait_ge(mixed if st.mix == "A" else exped, (st.mixes if st.mix == "A" else U) + u + 1)
                    if u >= (1 if st.mix in "CM" else 2):
                        transposed(u - (1 if st.mix in "CM" else 2))
                    banks = turn_banks(st, u)
                    n = 6 if st.mix == "C" else 2
                    for k in range(n):
                        b, o = divmod(k * P, BANK)
                        last = pe.transpose(bank[:, banks[b], o:o + P], probs[:, u % 2, k * P:(k + 1) * P], ident)
                    last.then_inc(probs_turned, 1)

                def weigh(u):
                    h, t = units[u]
                    d = 128 if st.mix == "A" else 64
                    per = BANK // d
                    o_banks = 1 if st.mix == "M" else 2
                    if u % per == 0 and u // per >= o_banks:
                        pe.wait_ge(o_out, st.obank + u // per - o_banks + 1)
                    transposed(u)
                    o = bank[:, 6 + (u // per) % o_banks, (u % per) * d:(u % per + 1) * d]
                    n = 6 if st.mix == "C" else 2
                    order = group_order(st, t)
                    for k in range(n):
                        g = order[k // 2]
                        v = V_B[:, k % 2, h * d:(h + 1) * d] if st.mix == "B" else V[:, g, k % 2, h * d:(h + 1) * d]
                        last = pe.matmul(o, probsT[:, u % 2, k, :], v, start=(k == 0), stop=(k == n - 1))
                    last.then_inc(o_done, 1)

                n = len(units)
                score(0)
                score(1)
                for u in range(n + 1):
                    if u < n:
                        turn(u)
                    if u + 2 < n:
                        score(u + 2)
                    if u >= 1:
                        weigh(u - 1)
                    beside(u)

            def acc_tile(at, k0, l_hi, l_lo, start, stop):
                weights(at)
                for kk in range(2):
                    for t in range(T2):
                        for half in range(2):
                            c = kk * D + half * BANK
                            last = product(bank[:, 2 * t + half, :], l_hi[:, k0 + kk, t * P:(t + 1) * P],
                                           l_lo[:, k0 + kk, t * P:(t + 1) * P],
                                           w_hi[:, at.slot, c:c + BANK], w_lo[:, at.slot, c:c + BANK],
                                           start=start and kk == 0, stop=stop and kk == 1)
                last.then_inc(w_used, 1)

            def hybrid_layer(st):
                operand_ready(st)
                at = Place(st.tile)

                def turn_slab(i, buf):
                    pe.wait_ge(slab_out, st.slab + i + 1)
                    if i == 2:
                        pe.wait_ge(turned_out, st.turned + 1)
                    for ft in range(4):
                        for t in range(T2):
                            b, o = divmod(ft * S + t * P, BANK)
                            last = pe.transpose(bank[:, 4 + 2 * (i % 2) + b, o:o + P],
                                                stage[:, buf, t, ft * P:(ft + 1) * P], ident)
                    last.then_inc(turned, 1)

                for i in range(4):
                    qkv_slab(at + 2 * i, st.slab + i, i % 2, True)
                    if i >= 1:
                        turn_slab(i - 1, (i - 1) % 2)

                def drive(i):
                    if i >= 2:
                        pe.wait_ge(v_used, i - 1)
                    p0 = (i % 4) * 32
                    for c in range(2):
                        last = pe.matmul(bank[:, 1 + 2 * (i % 2), c * S:(c + 1) * S], B_in[p0:p0 + 32, c, i // 4, :],
                                         uT[p0:p0 + 32, i // 4, :], start=True, stop=True)
                    last.then_inc(v_done, 1)

                def read_out(i):
                    pe.wait_ge(states, i + 1)
                    if i % 4 == 0 and i >= 8:
                        pe.wait_ge(y_out, i // 4 - 1)
                    p0 = (i % 4) * 32
                    o = bank[p0:p0 + 32, 5 + 2 * ((i // 4) % 2), 0:S]
                    for c in range(2):
                        last = pe.matmul(o, Cc[:, c, i, :], post_c[:, i % 2, c, :], start=(c == 0), stop=(c == 1))
                    last.then_inc(y_done, 1)

                def beside(u):
                    if u < STILES:
                        drive(u)
                    if u >= 2:
                        read_out(u - 2)

                pe.wait_ge(s5_in_done, 16)
                pe.wait_ge(pole_ready, 1)
                attend(st, beside)
                read_out(STILES - 1)
                pe.wait_ge(glu_hi, 1)
                pe.wait_ge(glu_lo, 1)
                weights(at + 8)
                sl = (at + 8).slot
                for e in range(4):
                    b = bank[:, e // 2, (e % 2) * S:(e % 2 + 1) * S]
                    for k in range(4):
                        w = slice(k * BANK + e * P, k * BANK + (e + 1) * P)
                        pe.matmul(b, w_hi[:, sl, w], xT_hi[:, k, :], start=(k == 0), stop=False)
                        pe.matmul(b, w_hi[:, sl, w], xT_lo[:, k, :], start=False, stop=False)
                        last = pe.matmul(b, w_lo[:, sl, w], xT_hi[:, k, :], start=False, stop=(k == 3))
                last.then_inc(w_used, 1)
                pe.wait_ge(hybrid_xs, 1)
                for k in range(4):
                    for t in range(T2):
                        o = (k % 2) * S + t * P
                        last = pe.transpose(bank[:, 4 + k // 2, o:o + P], xs[:, t, k * P:(k + 1) * P], ident)
                    if k % 2:
                        last.then_inc(op_turned, 1)
                pe.wait_ge(sq_done, 1)
                for k in range(4):
                    last = pe.matmul(bank[:, 2, 0:S], const_ap("ones"), y_sq[:, k, :], start=(k == 0), stop=(k == 3))
                last.then_inc(ss_done, 1)

            def out_projection(st):
                operand_ready(st)
                if st.post == "post_mix":
                    pe.wait_ge(mix_lo, 1)
                for i in range(4):
                    acc_tile(Place(st.tile + i), 2 * i, xT_hi, xT_lo, i == 0, i == 3)

            def ffn(st):
                operand_ready(st)
                C, J = st.chunk, st.pair

                def hidden(at, c, c_mod, check):
                    if check:
                        pe.wait_ge(h_done, c - 3)
                    weights(at)
                    for part in range(2):
                        for k in range(KD):
                            o = k * 2 * P + part * P
                            w = slice(o, o + P)
                            b = bank[:, 4 + c_mod, part * S:(part + 1) * S]
                            pe.matmul(b, w_hi[:, at.slot, w], xT_hi[:, k, :], start=(k == 0), stop=False)
                            pe.matmul(b, w_hi[:, at.slot, w], xT_lo[:, k, :], start=False, stop=False)
                            last = pe.matmul(b, w_lo[:, at.slot, w], xT_hi[:, k, :], start=False, stop=(k == KD - 1))
                    last.then_inc(w_used, 1)

                def down(at, j, buf, start, stop):
                    pe.wait_ge(h_lo, j + 1)
                    acc_tile(at, 0, hT_hi[:, buf, :, :], hT_lo[:, buf, :, :], start, stop)

                def pair(at, c, j, p, first, check):
                    hidden(at, c, (2 * p) % 4, check)
                    hidden(at + 1, c + 1, (2 * p + 1) % 4, check)
                    down(at + 2, j - 1, (p + 1) % 2, first, False)

                at = Place(st.tile)
                hidden(at, C, 0, False)
                hidden(at + 1, C + 1, 1, False)
                pair(at + 2, C + 2, J + 1, 1, True, False)
                pair(at + 5, C + 4, J + 2, 0, False, True)
                with pe.Fori(0, 3) as i:
                    for p in range(2):
                        pair(Place(st.tile + 8 + 3 * p, i * 2), i * 4 + (C + 6 + 2 * p), i * 2 + (J + 3 + p),
                             (1 + p) % 2, False, True)
                for p in range(2):
                    pair(at + 26 + 3 * p, C + 18 + 2 * p, J + 9 + p, (1 + p) % 2, False, True)
                down(at + 32, J + 10, 0, False, True)

            pe.sem_inc(w_used, RING)
            for st in stages:
                {"operand": operand, "qkv": qkv, "latent": latent, "lift": lift, "attend": attend,
                 "out": out_projection, "ffn": ffn, "norm": lambda s: None, "final_norm": lambda s: None,
                 "fetch": lambda s: None, "hybrid": hybrid_layer}[st.kind](st)


        @block.scalar
        def _(act):
            def hi_part(at):
                if type(at.count) is int and at.count >= tiles:
                    return
                act.wait_ge(tape_in[at.slot], at.round * 16 + 16)
                act.wait_ge(w_used, at.count + 1)
                act.activation(w_hi[:, at.slot, :], raw[:, at.slot, :], ACT.Copy).then_inc(hi_done, 1)

            def tile_done(at):
                act.wait_ge(w_used, at.count + RING + 1)

            def norm(st):
                act.wait_ge(x_in_done if st.norms == 0 else x_ready, 16 if st.norms == 0 else st.x_ready)
                act.activation(xs[:, 1, :], x[:, 1, :], ACT.Square, accum_out=stat[:, 0, 1:2]).then_inc(sq_act, 1)
                act.wait_ge(inv_ready, st.norms + 1)
                act.activation(xs[:, 1, :], x[:, 1, :], ACT.Copy, scale=stat[:, 2, 1:2]).then_inc(xs_act, 1)

            def operand(st):
                for b in range(-(-st.kts // 2)):
                    act.wait_ge(op_turned, st.operand + b + 1)
                    for k in range(2 * b, min(2 * b + 2, st.kts)):
                        src = bank[:, 4 + b, (k % 2) * S:(k % 2 + 1) * S]
                        g = 1.0 if st.gain is None else gain(st.gain, 0 if "subln" in st.gain else k)
                        last = act.activation(xT_hi[:, k, :], src, ACT.Copy, scale=g)
                    last.then_inc(op_hi, 1)

            def qkv_group(at, s0, t0, g, check):
                for s in range(6):
                    hi_part(at + (2 * s + LEAD))
                    hi_part(at + (2 * s + LEAD + 1))
                    tile_done(at + (2 * s + 1))
                    src = bank[:, 2 * (s % 2):2 * (s % 2) + 2, :]
                    if s < 4:
                        if check or s >= 2:
                            act.wait_ge(turned, t0 + (s - 1))
                        act.activation(stage[:, s % 2, :, :], src, ACT.Copy,
                                       scale=0.125 if s < 2 else 1.0).then_inc(slab_out, 1)
                    else:
                        o = V[:, bass.ds(g, 1), :, (s - 4) * BANK:(s - 3) * BANK].rearrange("p a t n -> p (a t) n") \
                            if type(g) is not int else V[:, g, :, (s - 4) * BANK:(s - 3) * BANK]
                        act.activation(o, src, ACT.Copy).then_inc(slab_out, 1)

            def qkv(st):
                if st.groups == 1:
                    qkv_group(Place(st.tile), st.slab, st.turned, 0, st.slab >= 2)
                else:
                    with act.Fori(0, st.groups) as g:
                        qkv_group(Place(st.tile, g * 4), g * 6 + st.slab, g * 4 + st.turned, g, True)

            def latent(st):
                at = Place(st.tile)
                hi_part(at + 2)
                hi_part(at + 3)
                tile_done(at + 1)
                act.activation(a_tm[:, :, 0:BANK], bank[:, 0:2, :], ACT.Copy).then_inc(slab_out, 1)
                hi_part(at + 4)
                tile_done(at + 2)
                act.activation(a_tm[:, :, BANK:672], bank[:, 2:4, 0:160], ACT.Copy).then_inc(slab_out, 1)

            def lift(st):
                at = Place(st.tile)
                k4 = k_tm[:, :, :].rearrange("p t (h d) -> p t h d", d=96)
                for i in range(7):
                    tile = at + (i if i < 3 else 3 + (i - 3) // 2)
                    if i < 3 or i % 2 == 1:
                        hi_part(tile + LEAD)
                    tile_done(tile)
                    src = bank[:, 2 * (i % 2):2 * (i % 2) + 2, :]
                    if i < 3:
                        act.activation(q_tm[:, :, i * BANK:(i + 1) * BANK], src, ACT.Copy,
                                       scale=float(np.float32(96.0) ** np.float32(-0.5))).then_inc(slab_out, 1)
                    elif i < 5:
                        for t in range(T2):
                            last = act.activation(k4[:, t, (i - 3) * 8:(i - 2) * 8, 0:64],
                                                  src[:, t, :].rearrange("p (h d) -> p h d", d=64), ACT.Copy)
                        last.then_inc(slab_out, 1)
                    else:
                        act.activation(V_B[:, :, (i - 5) * BANK:(i - 4) * BANK], src, ACT.Copy).then_inc(slab_out, 1)

            def attend(st):
                units = unit_list(st)
                n, U = len(units), st.unit

                def expo(u):
                    if u >= 2:
                        act.wait_ge(probs_turned, U + u - 1)
                    act.wait_ge(maxed, U + u + 1)
                    if st.mix == "A":
                        for sub in range(2):
                            last = act.activation(probs[:, u % 2, sub * S:(sub + 1) * S],
                                                  bank[:, 2 * (u % 2) + sub, 0:S], ACT.Exp,
                                                  bias=nmax[:, u % 2, sub:sub + 1], accum_out=sums[:, sub, u:u + 1])
                    else:
                        w = 768 if st.mix == "C" else S
                        src = bank[:, 2 * (u % 2), 0:S] if st.mix == "B" else probs[:, u % 2, 0:w]
                        last = act.activation(probs[:, u % 2, 0:w], src, ACT.Exp, bias=nmax[:, u % 2, 0:1],
                                              accum_out=sums[:, 0, u:u + 1])
                    last.then_inc(exped, 1)

                def copy_turned(u):
                    act.wait_ge(probs_turned, U + u + 1)
                    if u >= 2:
                        act.wait_ge(o_done, U + u - 1)
                    b = turn_banks(st, u)[-1]
                    k0 = 4 if st.mix == "C" else 0
                    act.activation(probsT[:, u % 2, k0:k0 + 2, :],
                                   bank[:, b, 0:S].rearrange("p (k q) -> p k q", q=P), ACT.Copy).then_inc(pt_act, 1)

                def squares(b):
                    act.wait_ge(o_out, st.obank + b + 1)
                    for u in range(4 * b, 4 * b + 4):
                        h, t = units[u]
                        last = act.activation(squared[:, u, :], xs[:, t, h * P:(h + 1) * P], ACT.Square,
                                              accum_out=stat[:, 0, t * 8 + h:t * 8 + h + 1])
                    last.then_inc(o_sq, 1)

                expo(0)
                for u in range(n):
                    if u + 1 < n:
                        expo(u + 1)
                    if st.mix in "AC":
                        copy_turned(u)
                    if st.mix == "A" and u % 4 == 1 and u >= 5:
                        squares(u // 4 - 1)
                if st.mix == "A":
                    squares(3)

            def fetch(st):
                act.wait_ge(x_ready, st.x_ready)
                act.dma_start(s5[:], s5_in).then_inc(s5_in_done, 16)
                act.dma_start(row[:], rows_in[0].partition_broadcast(P)).then_inc(row_in, 16)

            def fetch_row(n):
                act.wait_ge(row_used, n)
                act.dma_start(row[:], rows_in[n].partition_broadcast(P)).then_inc(row_in, 16)

            def hybrid_layer(st):
                at = Place(st.tile)
                fetch_row(1)
                act.activation(pole[:, 0, :], gains("log_dt"), ACT.Exp).then_inc(dt_ready, 1)
                act.wait_ge(mag_ready, 1)
                act.activation(pole[:, 2, :], pole[:, 1, :], ACT.Exp).then_inc(dt_ready, 1)
                act.wait_ge(angle_ready, 1)
                act.activation(trig_k[:, :, :, :], trig[:, :, :, :], ACT.Sin, scale=6.2831853).then_inc(trig_ready, 1)
                for i in range(4):
                    hi_part(at + (2 * i + LEAD))
                    hi_part(at + (2 * i + LEAD + 1))
                    tile_done(at + (2 * i + 1))
                    src = bank[:, 2 * (i % 2):2 * (i % 2) + 2, :]
                    if i == 2:
                        act.wait_ge(turned, st.turned + 1)
                    o = V[:, 0, :, 0:BANK] if i == 3 else stage[:, i % 2, :, :]
                    act.activation(o, src, ACT.Copy, scale=0.125 if i == 1 else 1.0).then_inc(slab_out, 1)
                attend(st)
                act.wait_ge(y_out, 4)
                act.activation(y_act[:, :, :], y_skip[:, :, :], ACT.Gelu_apprx_tanh).then_inc(gelu_done, 1)
                act.wait_ge(gelu_done, 1)
                act.activation(xT_hi[:, 0:4, :], y_act[:, :, :], ACT.Copy).then_inc(glu_hi, 1)
                hi_part(at + (8 + LEAD))
                tile_done(at + 8)
                for e in range(4):
                    last = act.activation(sig[:, e, :], bank[:, e // 2, (e % 2) * S:(e % 2 + 1) * S], ACT.Sigmoid,
                                          bias=gain("b_glu", e))
                last.then_inc(sig_done, 1)
                for b in range(2):
                    act.wait_ge(op_turned, st.operand + b + 1)
                    for k in (2 * b, 2 * b + 1):
                        last = act.activation(xT_hi[:, 4 + k, :], bank[:, 4 + b, (k % 2) * S:(k % 2 + 1) * S], ACT.Copy,
                                              scale=gain("attn_out", k))
                    last.then_inc(op_hi, 1)
                act.wait_ge(norm_done, 1)
                for k in range(4):
                    last = act.activation(xT_hi[:, k, :], y_norm[:, k, :], ACT.Copy, scale=gain("ssm_out", k))
                last.then_inc(mix_hi, 1)

            def out_projection(st):
                for i in range(4):
                    hi_part(Place(st.tile + i + LEAD))
                if st.post:
                    fetch_row(2)

            def ffn(st):
                C, J = st.chunk, st.pair

                def silu(at, c, c_mod, check):
                    tile_done(at)
                    if check:
                        act.wait_ge(h_done, c - 1)
                    act.activation(sg[:, c_mod % 2, :], bank[:, 4 + c_mod, 0:S], ACT.Silu).then_inc(silu_done, 1)

                def h_high(c, buf):
                    act.wait_ge(h_done, c + 2)
                    act.activation(hT_hi[:, buf, :, :], h32[:, buf, :, :], ACT.Copy).then_inc(h_hi, 1)

                def pair(at, c, p, check=True):
                    hi_part(at + LEAD)
                    silu(at, c, 2 * p, check)
                    hi_part(at + (LEAD + 1))
                    silu(at + 1, c + 1, 2 * p + 1, check)
                    if check:
                        hi_part(at + (LEAD + 2))
                    h_high(c, p)

                at = Place(st.tile)
                pair(at, C, 0, False)
                pair(at + 2, C + 2, 1)
                pair(at + 5, C + 4, 0)
                with act.Fori(0, 3) as i:
                    for p in range(2):
                        pair(Place(st.tile + 8 + 3 * p, i * 2), i * 4 + (C + 6 + 2 * p), (1 + p) % 2)
                for p in range(2):
                    pair(at + (26 + 3 * p), C + 18 + 2 * p, (1 + p) % 2)
                hi_part(at + (32 + LEAD))

            for n in range(LEAD):
                hi_part(Place(n))
            act.wait_ge(lam_dots, 1)
            act.activation(lam[:, 8:12], lam[:, 4:8], ACT.Exp).then_inc(lam_exp, 1)
            for st in stages:
                {"operand": operand, "qkv": qkv, "latent": latent, "lift": lift, "attend": attend,
                 "out": out_projection, "ffn": ffn, "norm": norm, "fetch": fetch, "final_norm": lambda s: None,
                 "hybrid": hybrid_layer}[st.kind](st)

        @block.vector
        def _(dve):
            links = [0]

            def link(ins):
                links[0] += 1
                ins.then_inc(chain, 1)
                dve.wait_ge(chain, links[0])

            def lo(at):
                if type(at.count) is int and at.count >= tiles:
                    return
                lo_part(dve, at, 0, SPLIT_DVE).then_inc(lo_dve, 1)

            def rsqrt(n, at=None):
                at = stat[:, 1:4, 0:n] if at is None else at
                v, y, a = at[:, 0, :], at[:, 1, :], at[:, 2, :]
                link(dve.tensor_scalar(a.bitcast(I32), v.bitcast(I32), 1, None, ALU.logical_shift_right))
                link(dve.tensor_scalar(y.bitcast(I32), a.bitcast(I32), -1.0, float(0x5F3759DF), ALU.mult, ALU.add))
                for step in range(3):
                    link(dve.scalar_tensor_tensor(a, y, -0.5, y, ALU.mult, ALU.mult))
                    link(dve.tensor_tensor(a, a, v, ALU.mult))
                    last = dve.scalar_tensor_tensor(y, a, 1.5, y, ALU.add, ALU.mult)
                    if step < 2:
                        link(last)
                return last

            def square_sum(src, width, col, junk):
                return dve.tensor_tensor_reduce(out=junk, in0=src, in1=src, scale=1.0, scalar=0.0, op0=ALU.mult,
                                                op1=ALU.add, accum_out=stat[:, 0, col:col + 1])

            def norm(st):
                if st.norms == 0:
                    dve.wait_ge(x_in_done, 16)
                link(square_sum(x[:, 0, :], D, 0, xs[:, 0, :]))
                dve.wait_ge(sq_act, st.norms + 1)
                link(dve.tensor_scalar(stat[:, 1, 0:2], stat[:, 0, 0:2], 1.0 / D, EPS, ALU.mult, ALU.add))
                rsqrt(2).then_inc(inv_ready, 1)
                dve.wait_ge(inv_ready, st.norms + 1)
                dve.tensor_scalar(xs[:, 0, :], x[:, 0, :], stat[:, 2, 0:1], None, ALU.mult).then_inc(xs_dve, 1)

            def operand(st):
                for b in range(-(-st.kts // 2)):
                    dve.wait_ge(op_hi, st.operand + b + 1)
                    for k in range(2 * b, min(2 * b + 2, st.kts)):
                        src = bank[:, 4 + b, (k % 2) * S:(k % 2 + 1) * S]
                        g = 1.0 if st.gain is None else gain(st.gain, 0 if "subln" in st.gain else k)
                        last = dve.scalar_tensor_tensor(xT_lo[:, k, :], src, g, xT_hi[:, k, :].bitcast(F32),
                                                        ALU.mult, ALU.subtract)
                    last.then_inc(op_lo, 1)

            def rotate(v, half, cos, sin, c1, c2):
                shape = list(v.shape)
                cb = cos.rearrange("p (t r) -> p t r", t=T2).unsqueeze(2).broadcast_to(shape)
                sb_ = sin.rearrange("p (t r) -> p t r", t=T2).unsqueeze(2).broadcast_to(shape)
                dve.tensor_tensor(c1, v, cb, ALU.mult)
                dve.tensor_tensor(c2[:, :, :, 0:half], v[:, :, :, half:], sb_[:, :, :, 0:half], ALU.mult)
                return dve.tensor_tensor(c2[:, :, :, half:], v[:, :, :, 0:half], sb_[:, :, :, half:], ALU.mult)

            def qkv_group(at, s0, r0, t0, g, check):
                for s in range(6):
                    lo(at + (2 * s + LEAD))
                    lo(at + (2 * s + LEAD + 1))
                    if s < 4:
                        dve.wait_ge(slab_out, s0 + (s + 1))
                        if check or s:
                            dve.wait_ge(rope_done, r0 + s)
                        v = stage[:, s % 2, :, :].rearrange("p t (h d) -> p t h d", d=64)[:, :, :, 0:16]
                        c1 = rot[:, 0, :].rearrange("p (t h d) -> p t h d", t=T2, d=16)
                        c2 = rot[:, 1, :].rearrange("p (t h d) -> p t h d", t=T2, d=16)
                        rotate(v, 8, const_ap("cos_a"), const_ap("sin_a"), c1, c2).then_inc(rope_mul, 1)
                        dve.wait_ge(rope_mul, r0 + (s + 1))
                        dve.tensor_tensor(v, c1, c2, ALU.add).then_inc(rope_done, 1)
                    if 1 <= s <= 4:
                        q = s - 1
                        dve.wait_ge(turned, t0 + (q + 1))
                        dst = QT if q < 2 else KT
                        b0 = 4 + 2 * (q % 2)
                        src = bank[:, b0:b0 + 2, :].rearrange("p b n -> p (b n)").rearrange("p (f n) -> p f n", n=S)
                        o = dst[:, g + (q % 2) * 4:g + (q % 2) * 4 + 4, :] if type(g) is int else \
                            dst[:, bass.ds(g + (q % 2) * 4, 4), :]
                        dve.tensor_copy(o, src).then_inc(turned_out, 1)

            def qkv(st):
                if st.groups == 1:
                    qkv_group(Place(st.tile), st.slab, st.rope, st.turned, 0, st.slab >= 2)
                else:
                    with dve.Fori(0, st.groups) as g:
                        qkv_group(Place(st.tile, g * 4), g * 6 + st.slab, g * 4 + st.rope, g * 4 + st.turned,
                                  g * 8, True)

            def latent(st):
                for i in range(3):
                    lo(Place(st.tile + i + LEAD))
                dve.wait_ge(slab_out, st.slab + 2)
                parts = [(0, 384), (384, 640)]
                for i, (a, b) in enumerate(parts):
                    for t in range(T2):
                        last = square_sum(a_tm[:, t, a:b], b - a, 2 * i + t, xs[:, t, a:b])
                link(last)
                for i, (a, b) in enumerate(parts):
                    last = dve.tensor_scalar(stat[:, 1, 2 * i:2 * i + 2], stat[:, 0, 2 * i:2 * i + 2], 1.0 / (b - a),
                                             EPS, ALU.mult, ALU.add)
                link(last)
                link(rsqrt(4))
                kr = a_tm[:, :, 640:672].unsqueeze(2)
                c1 = rot[:, 0, 0:64].rearrange("p (t h d) -> p t h d", t=T2, h=1)
                c2 = rot[:, 1, 0:64].rearrange("p (t h d) -> p t h d", t=T2, h=1)
                link(rotate(kr, 16, const_ap("cos_b"), const_ap("sin_b"), c1, c2))
                dve.tensor_tensor(kr, c1, c2, ALU.add)
                for i, (a, b) in enumerate(parts):
                    for t in range(T2):
                        last = dve.tensor_scalar(a_tm[:, t, a:b], a_tm[:, t, a:b],
                                                 stat[:, 2, 2 * i + t:2 * i + t + 1], None, ALU.mult)
                last.then_inc(lat_ready, 1)
                dve.wait_ge(lat_ready, 1)

            def lift(st):
                for i in range(3):
                    lo(Place(st.tile + i + LEAD))
                dve.wait_ge(slab_out, st.slab + 3)
                v = q_tm[:, :, :].rearrange("p t (h d) -> p t h d", d=96)[:, :, :, 64:96]
                c1 = xs[:, 0, :].rearrange("p (t h d) -> p t h d", t=T2, d=32)
                c2 = xs[:, 1, :].rearrange("p (t h d) -> p t h d", t=T2, d=32)
                link(rotate(v, 16, const_ap("cos_b"), const_ap("sin_b"), c1, c2))
                dve.tensor_tensor(v, c1, c2, ALU.add).then_inc(lat_ready, 1)
                lo(Place(st.tile + 3 + LEAD))
                k4 = k_tm[:, :, :].rearrange("p t (h d) -> p t h d", d=96)
                for t in range(T2):
                    last = dve.tensor_copy(k4[:, t, :, 64:96],
                                           a_tm[:, t, 640:672].unsqueeze(1).broadcast_to([P, 16, 32]))
                last.then_inc(lat_ready, 1)
                lo(Place(st.tile + 4 + LEAD))
                for i in range(8):
                    dve.wait_ge(turned, st.turned + i + 1)
                    b0 = 4 + 2 * (i % 2)
                    dst = QB if i < 4 else KB
                    dve.tensor_copy(dst[:, (i % 4) * 4:(i % 4) * 4 + 4, :],
                                    bank[0:96, b0:b0 + 2, :].rearrange("p b n -> p (b n)")
                                    .rearrange("p (f n) -> p f n", n=S)).then_inc(turned_out, 1)

            def attend(st, beside=lambda u: None):
                units = unit_list(st)
                n, U = len(units), st.unit
                d = P if st.mix == "A" else 64
                per = BANK // d

                def maximum(u):
                    dve.wait_ge(scores, U + u + 1)
                    if u >= 2:
                        dve.wait_ge(exped, U + u - 1)
                    h, t = units[u]
                    if st.mix in "AB":
                        subs = 2 if st.mix == "A" else 1
                        src = bank[:, 2 * (u % 2):2 * (u % 2) + subs, 0:S]
                        dve.tensor_reduce(nmax[:, u % 2, 0:subs], src, AX_X, ALU.max, negate=True).then_inc(maxed, 1)
                        return
                    if u >= 2:
                        dve.wait_ge(probs_turned, U + u - 1)
                    w = 768 if st.mix == "C" else S
                    b = 2 * (u % 2)
                    src = bank[:, b:b + 2, :].rearrange("p b n -> p (b n)")[:, 0:w]
                    o = (t * S if st.mix == "C" else (1 - t) * P)
                    m = const_ap("mask" if st.mix == "C" else "causal")[:, o:o + w]
                    link(dve.tensor_tensor_reduce(out=probs[:, u % 2, 0:w], in0=src, in1=m, scale=1.0, scalar=LOWEST,
                                                  op0=ALU.add, op1=ALU.max, accum_out=nmax[:, u % 2, 1:2]))
                    dve.tensor_scalar(nmax[:, u % 2, 0:1], nmax[:, u % 2, 1:2], -1.0, None, ALU.mult
                                      ).then_inc(maxed, 1)

                def mix(u):
                    dve.wait_ge(exped, U + u + 1)
                    r = stat[:, 4, 0:1]
                    link(dve.reciprocal(r, sums[:, 1, u:u + 1]))
                    link(dve.scalar_tensor_tensor(stat[:, 4, 1:2], r, sums[:, 0, u:u + 1], lam[:, st.j:st.j + 1],
                                                  ALU.mult, ALU.mult))
                    dve.scalar_tensor_tensor(probs[:, u % 2, 0:S], probs[:, u % 2, S:2 * S], stat[:, 4, 1:2],
                                             probs[:, u % 2, 0:S], ALU.mult, ALU.add).then_inc(mixed, 1)

                def copy_turned(u):
                    dve.wait_ge(probs_turned, U + u + 1)
                    if u >= 2:
                        dve.wait_ge(o_done, U + u - 1)
                    k = 4 if st.mix == "C" else 2
                    dve.tensor_copy(probsT[:, u % 2, 0:k, :],
                                    bank[:, turn_banks(st, u)[0], 0:k * P].rearrange("p (k q) -> p k q", q=P)
                                    ).then_inc(pt_dve, 1)

                def result(b):
                    dve.wait_ge(o_done, U + (b + 1) * per)
                    inv = stat[:, 4, 8:8 + per]
                    link(dve.reciprocal(inv, sums[:, 0, b * per:(b + 1) * per]))
                    hs = per // 2
                    w = hs * d
                    o = xs[:, :, b * w:(b + 1) * w].rearrange("p t (h d) -> p h t d", d=d)
                    src = bank[:, 6 + (0 if st.mix == "M" else b % 2), :].rearrange("p (h t d) -> p h t d", t=T2, d=d)
                    dve.tensor_tensor(o, src, inv.rearrange("p (h t) -> p h t", t=T2).unsqueeze(3)
                                      .broadcast_to([P, hs, T2, d]), ALU.mult).then_inc(o_out, 1)

                maximum(0)
                for u in range(n):
                    if u + 1 < n:
                        maximum(u + 1)
                    if st.mix == "A":
                        mix(u)
                    if st.mix != "A":
                        copy_turned(u)
                    if u % per == 0 and u:
                        result(u // per - 1)
                    beside(u)
                result(n // per - 1)
                if st.mix == "A":
                    dve.wait_ge(o_sq, 4 * (st.j + 1))
                    link(dve.tensor_scalar(stat[:, 1, 0:16], stat[:, 0, 0:16], 1.0 / P, EPS, ALU.mult, ALU.add))
                    link(rsqrt(16))
                    v = xs[:, :, :].rearrange("p t (h d) -> p (t h) d", d=P)
                    dve.tensor_tensor(v, v, stat[:, 2, 0:16].unsqueeze(2).broadcast_to([P, 16, P]), ALU.mult
                                      ).then_inc(xs_dve, 1)

            def inverse_rms(width):
                link(dve.tensor_scalar(stat[:, 1, 0:2], stat[:, 0, 0:2], 1.0 / width, EPS, ALU.mult, ALU.add))
                link(rsqrt(2))

            def final_norm(st):
                for t in range(T2):
                    last = square_sum(x[:, t, :], D, t, xs[:, t, :])
                link(last)
                inverse_rms(D)
                dve.wait_ge(row_in, 16)
                for t in range(T2):
                    last = dve.scalar_tensor_tensor(x[:, t, :], x[:, t, :], stat[:, 2, t:t + 1], row[:, :],
                                                    ALU.mult, ALU.mult)
                last.then_inc(row_used, 1)
                dve.wait_ge(row_used, 1)
                dve.sem_inc(x_ready, 1)

            def wrap(dst, src, tmp, add=0.0, scale=1.0):
                link(dve.tensor_scalar(dst, src, scale, add, ALU.mult, ALU.add))
                link(dve.tensor_scalar(tmp, dst, MAGIC, None, ALU.add))
                link(dve.tensor_scalar(tmp, tmp, MAGIC, None, ALU.subtract))
                link(dve.tensor_tensor(dst, dst, tmp, ALU.subtract))

            def poles(st):
                dt, ad, mag, ang, tmp, cr, ci, den, nr, li, m2, t3 = (pole[:, i, :] for i in range(12))
                re, im = gains("a_re"), gains("a_im")
                dve.wait_ge(dt_ready, 1)
                dve.tensor_tensor(ad, re, dt, ALU.mult).then_inc(mag_ready, 1)
                link(dve.tensor_tensor(ang, im, dt, ALU.mult))
                link(dve.tensor_scalar(tmp, ang, 1.0 / TURN, MAGIC, ALU.mult, ALU.add))
                link(dve.tensor_scalar(tmp, tmp, MAGIC, None, ALU.subtract))
                link(dve.scalar_tensor_tensor(ang, tmp, -TURN_HI, ang, ALU.mult, ALU.add))
                link(dve.scalar_tensor_tensor(ang, tmp, -TURN_LO, ang, ALU.mult, ALU.add))
                wrap(trig[:, 0, 0, :], ang, tmp, scale=1.0 / TURN)
                for k in range(1, SHIFTS):
                    wrap(trig[:, 0, k, :], trig[:, 0, k - 1, :], tmp, scale=2.0)
                sines = trig[:, 0, :, :].rearrange("p k n -> p (k n)")
                cosines = trig[:, 1, :, :].rearrange("p k n -> p (k n)")
                wrap(cosines, sines, E_re[:, 0, 0:SHIFTS * STILES], add=0.25)
                link(dve.tensor_scalar(trig[:, :, :, :], trig[:, :, :, :], 0.4999999, -0.4999999, ALU.min, ALU.max))
                dve.sem_inc(angle_ready, 1)
                dve.wait_ge(trig_ready, 1)
                dve.wait_ge(dt_ready, 2)
                link(dve.tensor_tensor(nr, mag, trig_k[:, 1, 0, :], ALU.mult))
                dve.tensor_scalar(nr, nr, -1.0, None, ALU.add)
                dve.tensor_tensor(li, mag, trig_k[:, 0, 0, :], ALU.mult)
                dve.tensor_tensor(den, re, re, ALU.mult)
                link(dve.tensor_tensor(m2, im, im, ALU.mult))
                link(dve.tensor_tensor(den, den, m2, ALU.add))
                link(dve.reciprocal(den, den))
                dve.tensor_tensor(cr, nr, re, ALU.mult)
                dve.tensor_tensor(m2, li, im, ALU.mult)
                dve.tensor_tensor(ci, li, re, ALU.mult)
                link(dve.tensor_tensor(t3, nr, im, ALU.mult))
                dve.tensor_tensor(cr, cr, m2, ALU.add)
                link(dve.tensor_tensor(ci, ci, t3, ALU.subtract))
                dve.tensor_tensor(cr, cr, den, ALU.mult)
                link(dve.tensor_tensor(ci, ci, den, ALU.mult))

            def output_factors():
                dve.wait_ge(s5_in_done, 16)
                shape = [P, STILES, 32]
                cr = pole[:, 5, :].unsqueeze(2).broadcast_to(shape)
                ci = pole[:, 6, :].unsqueeze(2).broadcast_to(shape)
                a, b = (q_tmp[:, i, :].rearrange("p (n h) -> p n h", h=32) for i in range(2))
                dve.tensor_tensor(a, C_in[:, 0, :, :], cr, ALU.mult)
                link(dve.tensor_tensor(b, C_in[:, 1, :, :], ci, ALU.mult))
                link(dve.tensor_tensor(Cc[:, 0, :, :], a, b, ALU.subtract))
                dve.tensor_tensor(a, C_in[:, 0, :, :], ci, ALU.mult)
                link(dve.tensor_tensor(b, C_in[:, 1, :, :], cr, ALU.mult))
                dve.scalar_tensor_tensor(Cc[:, 1, :, :], a, -1.0, b, ALU.mult, ALU.subtract).then_inc(pole_ready, 1)

            def phase_tables(k):
                n = 2 ** k
                shape = [P, STILES, n]
                c = trig_k[:, 1, k, :].unsqueeze(2).broadcast_to(shape)
                s_ = trig_k[:, 0, k, :].unsqueeze(2).broadcast_to(shape)
                tmp = xs[:, :, :].rearrange("p t d -> p (t d)")[:, 0:STILES * n].rearrange("p (i n) -> p i n", i=STILES)
                old_r, old_i = E_re[:, :, 0:n], E_im[:, :, 0:n]
                new_r, new_i = E_re[:, :, n:2 * n], E_im[:, :, n:2 * n]
                dve.tensor_tensor(new_r, old_r, c, ALU.mult)
                link(dve.tensor_tensor(tmp, old_i, s_, ALU.mult))
                link(dve.tensor_tensor(new_r, new_r, tmp, ALU.subtract))
                dve.tensor_tensor(new_i, old_i, c, ALU.mult)
                link(dve.tensor_tensor(tmp, old_r, s_, ALU.mult))
                link(dve.tensor_tensor(new_i, new_i, tmp, ALU.add))

            def hybrid_layer(st):
                at = Place(st.tile)
                poles(st)
                lo(at + LEAD)
                output_factors()
                dve.memset(E_re[:, :, 0:1], 1.0)
                link(dve.memset(E_im[:, :, 0:1], 0.0))
                for k in range(5):
                    phase_tables(k)
                for i in range(4):
                    if i:
                        lo(at + (2 * i + LEAD))
                    lo(at + (2 * i + LEAD + 1))
                    if i < 3:
                        phase_tables(5 + i)
                    if i >= 1:
                        dve.wait_ge(turned, st.turned + i)
                        dst = (None, uT[:, :, :], QT[:, 0:4, :], KT[:, 0:4, :])[i]
                        b0 = 4 + 2 * ((i - 1) % 2)
                        src = bank[:, b0:b0 + 2, :].rearrange("p b n -> p (b n)").rearrange("p (f n) -> p f n", n=S)
                        dve.tensor_copy(dst, src).then_inc(turned_out, 1)

                def to_states(i):
                    er = E_re[:, i, :].unsqueeze(1).broadcast_to([P, 2, S])
                    ei = E_im[:, i, :].unsqueeze(1).broadcast_to([P, 2, S])
                    v = bank[:, 1 + 2 * (i % 2), :].rearrange("p (c n) -> p c n", c=2)
                    dve.wait_ge(v_done, i + 1)
                    if i >= 1:
                        dve.wait_ge(scanned, i)
                    if i >= 2:
                        dve.wait_ge(states, i - 1)
                    dve.tensor_tensor(pre_c[:, :, :], v, er, ALU.mult)
                    dve.tensor_tensor(pre_s[:, :, :], v, ei, ALU.mult).then_inc(v_used, 1)
                    dve.wait_ge(v_used, i + 1)
                    dve.tensor_tensor(pre_c[:, 0, :], pre_c[:, 0, :], pre_s[:, 1, :], ALU.add)
                    link(dve.tensor_tensor(pre_c[:, 1, :], pre_c[:, 1, :], pre_s[:, 0, :], ALU.subtract))
                    radius = pole[:, 2, i:i + 1].broadcast_to([P, S])
                    for c in range(2):
                        last = dve.tensor_tensor_scan(scan[:, i % 2, c, :], radius, pre_c[:, c, :], 0.0,
                                                      ALU.mult, ALU.add)
                    last.then_inc(scanned, 1)

                def outputs(f):
                    dve.wait_ge(y_done, 4 * f + 4)
                    dve.scalar_tensor_tensor(y_skip[:, f, :], uT[:, f, :], gain("ssm_d", f),
                                             bank[:, 5 + 2 * (f % 2), 0:S], ALU.mult, ALU.add).then_inc(y_out, 1)

                def beside(u):
                    to_states(u)
                    if u >= 7 and u % 4 == 3:
                        outputs(u // 4 - 1)

                attend(st, beside)
                outputs(3)
                dve.wait_ge(gelu_done, 1)
                dve.wait_ge(glu_hi, 1)
                dve.tensor_tensor(xT_lo[:, 0:4, :], y_act[:, :, :], xT_hi[:, 0:4, :].bitcast(F32), ALU.subtract
                                  ).then_inc(glu_lo, 1)
                lo(at + (8 + LEAD))
                for t in range(T2):
                    last = square_sum(xs[:, t, 0:BANK], BANK, t, xs[:, t, BANK:])
                link(last)
                inverse_rms(BANK)
                for t in range(T2):
                    last = dve.tensor_scalar(xs[:, t, 0:BANK], xs[:, t, 0:BANK], stat[:, 2, t:t + 1], None, ALU.mult)
                last.then_inc(hybrid_xs, 1)
                dve.wait_ge(sig_done, 1)
                link(dve.tensor_tensor(y_gated[:, :, :], y_act[:, :, :], sig[:, :, :], ALU.mult))
                dve.tensor_tensor(y_sq[:, :, :], y_gated[:, :, :], y_gated[:, :, :], ALU.mult).then_inc(sq_done, 1)
                for b in range(2):
                    dve.wait_ge(op_hi, st.operand + b + 1)
                    for k in (2 * b, 2 * b + 1):
                        last = dve.scalar_tensor_tensor(xT_lo[:, 4 + k, :], bank[:, 4 + b, (k % 2) * S:(k % 2 + 1) * S],
                                                        gain("attn_out", k), xT_hi[:, 4 + k, :].bitcast(F32),
                                                        ALU.mult, ALU.subtract)
                    last.then_inc(op_lo, 1)
                dve.wait_ge(ss_done, 1)
                link(dve.tensor_scalar(inv3[:, 0, :], bank[:, 2, 0:S], 1.0 / BANK, EPS, ALU.mult, ALU.add))
                link(rsqrt(S, inv3))
                dve.tensor_tensor(y_norm[:, :, :], y_gated[:, :, :],
                                  inv3[:, 1, :].unsqueeze(1).broadcast_to([P, 4, S]), ALU.mult).then_inc(norm_done, 1)
                dve.wait_ge(mix_hi, 1)
                for k in range(4):
                    last = dve.scalar_tensor_tensor(xT_lo[:, k, :], y_norm[:, k, :], gain("ssm_out", k),
                                                    xT_hi[:, k, :].bitcast(F32), ALU.mult, ALU.subtract)
                last.then_inc(mix_lo, 1)

            def residual(st, last_tile):
                dve.wait_ge(w_used, last_tile + 1 + RING)
                if st.post:
                    for t in range(T2):
                        last = dve.tensor_copy(xs[:, t, :], bank[:, 2 * t:2 * t + 2, :].rearrange("p b n -> p (b n)"))
                    link(last)
                    for t in range(T2):
                        last = square_sum(xs[:, t, :], D, t, h_junk[:, t, :])
                    link(last)
                    inverse_rms(D)
                    dve.wait_ge(row_in, 16 * (st.rows + 1))
                    for t in range(T2):
                        last = dve.scalar_tensor_tensor(xs[:, t, :], xs[:, t, :], stat[:, 2, t:t + 1], row[:, :],
                                                        ALU.mult, ALU.mult)
                    last.then_inc(row_used, 1)
                    dve.wait_ge(row_used, st.rows + 1)
                    for t in range(T2):
                        last = dve.tensor_tensor(x[:, t, :], xs[:, t, :], x[:, t, :], ALU.add)
                    last.then_inc(x_ready, 1)
                    dve.wait_ge(x_ready, st.x_ready + 1)
                    return
                for t in range(T2):
                    last = dve.tensor_tensor(x[:, t, :], bank[:, 2 * t:2 * t + 2, :].rearrange("p b n -> p (b n)"),
                                             x[:, t, :], ALU.add)
                last.then_inc(x_ready, 1)
                dve.wait_ge(x_ready, st.x_ready + 1)

            def out_projection(st):
                for i in range(4):
                    lo(Place(st.tile + i + LEAD))
                residual(st, st.tile + 3)

            def ffn(st):
                C, J = st.chunk, st.pair

                def hidden(at, c, c_mod, p):
                    dve.wait_ge(silu_done, c + 1)
                    dve.tensor_tensor(h32[:, p, c_mod % 2, :], bank[:, 4 + c_mod, S:2 * S], sg[:, c_mod % 2, :],
                                      ALU.mult).then_inc(h_done, 1)

                def pair(at, c, j, p, three=True):
                    lo(at + LEAD)
                    hidden(at, c, 2 * p, p)
                    lo(at + (LEAD + 1))
                    hidden(at + 1, c + 1, 2 * p + 1, p)
                    if three:
                        lo(at + (LEAD + 2))
                    dve.wait_ge(h_hi, j + 1)
                    dve.tensor_tensor(hT_lo[:, p, :, :], h32[:, p, :, :], hT_hi[:, p, :, :].bitcast(F32),
                                      ALU.subtract).then_inc(h_lo, 1)

                at = Place(st.tile)
                pair(at, C, J, 0, False)
                pair(at + 2, C + 2, J + 1, 1)
                pair(at + 5, C + 4, J + 2, 0)
                with dve.Fori(0, 3) as i:
                    for p in range(2):
                        pair(Place(st.tile + 8 + 3 * p, i * 2), i * 4 + (C + 6 + 2 * p), i * 2 + (J + 3 + p),
                             (1 + p) % 2)
                for p in range(2):
                    pair(at + (26 + 3 * p), C + 18 + 2 * p, J + 9 + p, (1 + p) % 2)
                lo(at + (32 + LEAD))
                residual(st, st.tile + 32)

            for n in range(LEAD):
                lo(Place(n))
            dve.wait_ge(small_in, 48)
            v = V[:, 0, 0, 0:512].rearrange("p (w s n) -> p w s n", w=2, s=2)
            prod = V[:, 0, 1, 0:256].rearrange("p (w n) -> p w n", w=2)
            link(dve.tensor_tensor(prod, v[:, :, 0, :], v[:, :, 1, :], ALU.mult))
            dve.tensor_reduce(lam[:, 4:8], V[:, 0, 1, 0:256].rearrange("p (a n) -> p a n", n=64), AX_X, ALU.add
                              ).then_inc(lam_dots, 1)
            dve.wait_ge(lam_exp, 1)
            link(dve.tensor_tensor(lam[:, 0:2], lam[:, 10:12], lam[:, 8:10], ALU.subtract))
            for j in range(2):
                dve.tensor_scalar(lam[:, j:j + 1], lam[:, j:j + 1], -lambda_init(3 * j), None, ALU.add)
                g = gain(f"subln{j}", 0)
                last = dve.tensor_scalar(g, g, 1.0 - lambda_init(3 * j), None, ALU.mult)
            link(last)
            for st in stages:
                {"operand": operand, "qkv": qkv, "latent": latent, "lift": lift, "attend": attend,
                 "out": out_projection, "ffn": ffn, "norm": norm, "fetch": lambda s: None,
                 "final_norm": final_norm, "hybrid": hybrid_layer}[st.kind](st)
            dve.sem_inc(out_ready, 1)


def constants():
    c = np.zeros((P, CONST_W), np.float32)

    def put(name, v):
        o, w = CONST[name]
        c[:, o:o + w] = v.reshape(P, w)

    put("ones", np.ones((P, P), np.float32))
    put("ident", np.eye(P, dtype=np.float32))
    for name, rot in (("a", 16), ("b", 32)):
        pos = np.arange(S, dtype=np.float32)
        inv = np.float32(500000.0) ** (-np.arange(0, rot, 2, dtype=np.float32) / np.float32(rot))
        ang = (pos[:, None] * inv[None, :].astype(np.float32)).astype(np.float32)
        cos, sin = np.cos(ang), np.sin(ang)
        put(f"cos_{name}", np.concatenate([cos, cos], 1).reshape(T2, P, rot).transpose(1, 0, 2))
        put(f"sin_{name}", np.concatenate([-sin, sin], 1).reshape(T2, P, rot).transpose(1, 0, 2))
    i = np.arange(P)[:, None]
    k = np.arange(S)[None, :]
    off = np.float32(-1e30)

    def mask(keep):
        return np.where(keep, np.float32(0.0), off)

    put("mask", np.concatenate([mask(abs(i - k) <= 64), mask((i - k) % 4 == 0), mask((i - k) % 16 == 0),
                                mask(abs(i + P - k) <= 64)], 1))
    put("causal", mask(np.arange(384)[None, :] <= i + P))
    return c


def put_tiles(tape, at, block):
    tape[at:at + block.shape[0], :, :block.shape[2]] = block
    return at + block.shape[0]


def slabs(w):
    n = w.shape[1] // BANK
    return w.reshape(2, 4, P, n, BANK).transpose(3, 0, 2, 1, 4).reshape(2 * n, P, 4 * BANK)


def out_tiles(w):
    return w.reshape(-1, 2, P, D).transpose(0, 2, 1, 3).reshape(-1, P, 2 * D)


def put_ffn(tape, at, gate, up, down):
    gu = np.stack([gate, up], 1).reshape(KD, P, 2, CHUNKS, P).transpose(3, 1, 0, 2, 4).reshape(CHUNKS, P, TILE)
    dn = out_tiles(down)
    order = [gu[0], gu[1]]
    for j in range(1, CHUNKS // 2):
        order += [gu[2 * j], gu[2 * j + 1], dn[j - 1]]
    order.append(dn[-1])
    for t in order:
        tape[at] = t
        at += 1
    return at


def layout(w):
    tape = np.zeros((plan()[1], P, TILE), np.float32)
    at = 0
    for layer in LAYERS:
        j = layer // 3
        if layer % 3 == 0:
            at = put_tiles(tape, at, slabs(w["a_w_qkv"][j]))
            at = put_tiles(tape, at, out_tiles(w["a_w_o"][j]))
        elif layer % 3 == 1:
            a = w["b_w_a"][j]
            at = put_tiles(tape, at, slabs(a[:, :BANK]))
            at = put_tiles(tape, at, a[:, BANK:].reshape(1, KD, P, 160).transpose(0, 2, 1, 3).reshape(1, P, KD * 160))
            at = put_tiles(tape, at, w["b_w_qb"][j].reshape(3, P, 3, BANK).transpose(2, 1, 0, 3).reshape(3, P, 3 * BANK))
            kv = w["b_w_kvb"][j].reshape(2, P, 16, 2, 64).transpose(3, 1, 0, 2, 4).reshape(2, P, 2 * D)
            at = put_tiles(tape, at, kv)
            at = put_tiles(tape, at, out_tiles(w["b_w_o"][j]))
        else:
            at = put_tiles(tape, at, slabs(w["c_w_qkv"][j]))
            at = put_tiles(tape, at, out_tiles(w["c_w_o"][j]))
        gu = w["f_w_gu"][layer]
        at = put_ffn(tape, at, gu[:, :FFN], gu[:, FFN:], w["f_w_out"][layer])
    at = put_tiles(tape, at, slabs(w["w_in_2"][0]))
    at = put_tiles(tape, at, w["w_glu_2"][0].reshape(1, 4, P, BANK).transpose(0, 2, 1, 3).reshape(1, P, 4 * BANK))
    at = put_tiles(tape, at, out_tiles(w["w_out_2"][0]))
    at = put_ffn(tape, at, w["w_gate_2"][0], w["w_up_2"][0], w["w_down_2"][0])
    assert at == tape.shape[0]
    small = np.zeros((P, SMALL_W), np.float32)

    def col(name, v):
        o, width = SMALL[name]
        small[:, o:o + width] = v.reshape(width, P).T

    for layer in range(4):
        col(f"attn_norm{layer}", w["attn_norm"][layer])
        col(f"ffn_norm{layer}", w["ffn_norm"][layer])
    col("lat", np.concatenate([w["b_q_norm"][0], w["b_kv_norm"][0]]))
    for j in range(2):
        col(f"subln{j}", w["a_subln"][j])
    col("pre_mix", w["g_pre_mix_2"][0])
    col("pre_ffn", w["g_pre_ffn_2"][0])
    col("ssm_out", w["g_ssm_out_2"][0])
    col("attn_out", w["g_attn_out_2"][0])
    col("b_glu", w["b_glu_2"][0])
    col("ssm_d", w["ssm_d_2"][0])
    col("a_re", w["ssm_a_re_2"][0])
    col("a_im", w["ssm_a_im_2"][0])
    col("log_dt", np.repeat(w["ssm_log_dt_2"][0], STATES))
    s5 = np.zeros((P, S5_W), np.float32)
    b_in = s5[:, :1024].reshape(P, 2, 4, P)
    c_in = s5[:, 1024:].reshape(P, 2, STILES, 32)
    for c, name in enumerate(("re", "im")):
        b, cc = w[f"ssm_b_{name}_2"][0], w[f"ssm_c_{name}_2"][0]
        for g in range(GROUPS):
            i, odd = divmod(g, 2)
            f = (i % 4) * 32 + odd * GIN
            b_in[f:f + GIN, c, i // 4, odd * STATES:(odd + 1) * STATES] = b[g].T
            c_in[odd * STATES:(odd + 1) * STATES, c, i, odd * GIN:(odd + 1) * GIN] = cc[g].T
    return tape, small, s5


def kernel(**inputs):
    import concourse.bacc as bacc
    from concourse.bass_utils import run_bass_kernel_spmd

    w = {n: np.asarray(v) for n, v in inputs.items()}
    tape, small, s5 = layout(w)
    lam = np.concatenate([w[f"a_lambda_{n}"].reshape(-1) for n in ("q1", "k1", "q2", "k2")])
    arrays = {"x_dram": w["x"][0], "tape_dram": tape, "small_dram": small, "const_dram": constants(),
              "lam_dram": lam, "rows_dram": np.stack([w["final_norm"], w["g_post_mix_2"][0], w["g_post_ffn_2"][0]]), "s5_dram": s5}
    nc = bacc.Bacc("TRN2", target_bir_lowering=False, num_devices=1)
    args = [nc.dram_tensor(n, a.shape, F32, kind="ExternalInput").ap() for n, a in arrays.items()]
    out = nc.dram_tensor("out_dram", (S, D), F32, kind="ExternalOutput").ap()
    build_program(nc, *args, out)
    r = run_bass_kernel_spmd(nc, [arrays], core_ids=[0])
    return r.results[0]["out_dram"].reshape(1, S, D)
```

```python
from contextlib import ExitStack

import numpy as np

import concourse.bass as bass
from concourse import mybir

F32 = mybir.dt.float32
F32R = mybir.dt.float32r
I32 = mybir.dt.int32
ALU = mybir.AluOpType
ACT = mybir.ActivationFunctionType
AX_X = mybir.AxisListType.X

P = 128
S = 256
T2 = S // P
D = 1024
KD = D // P
BANK = 512
FFN = 2816
CHUNKS = FFN // P
EPS = 1e-6
TILE = 2048
RING = 3
LEAD = 2
SPLIT_DVE = 1024
LOWEST = -3.0e38
MAGIC = 12582912.0
TURN = 6.283185307179586
TURN_HI = 6.28125
TURN_LO = TURN - TURN_HI


class Place:

    def __init__(self, base, turns=0):
        self.base, self.turns = base, turns

    def __add__(self, n):
        return Place(self.base + n, self.turns)

    @property
    def slot(self):
        return self.base % RING

    @property
    def count(self):
        return self.turns * RING + self.base

    @property
    def round(self):
        return self.turns + self.base // RING


LAYERS = (0, 1, 2, 3)


def lambda_init(layer):
    return 0.8 - 0.6 * float(np.exp(-0.3 * layer))


class Stage:

    def __init__(self, kind, at, src="xs", kts=KD, gain=None, groups=1, mix=None, j=0, post=None):
        self.kind, self.src, self.kts, self.gain = kind, src, kts, gain
        self.groups, self.mix, self.j, self.post = groups, mix, j, post
        self.tile, self.slab, self.rope, self.turned = at["tile"], at["slab"], at["rope"], at["turned"]
        self.unit, self.mixes, self.split, self.values = at["unit"], at["mixes"], at["split"], at["values"]
        self.feature_turn, self.scaled = at["feature_turn"], at["scaled"]
        self.obank, self.operand, self.chunk, self.pair = at["obank"], at["operand"], at["chunk"], at["pair"]
        self.norms, self.xsd, self.x_ready, self.rows = at["norms"], at["xsd"], at["x_ready"], at["rows"]


def plan():
    stages = []
    c = dict(tile=0, slab=0, rope=0, turned=0, unit=0, mixes=0, split=0, values=0, obank=0, operand=0,
             chunk=0, pair=0, norms=0, xsd=0, feature_turn=0, scaled=0, x_ready=0, rows=0)

    def add(kind, uses, **k):
        stages.append(Stage(kind, c, **k))
        for n, v in uses.items():
            c[n] += v

    for layer in LAYERS:
        mixer = ("A", "B", "C")[layer % 3]
        add("norm", dict(norms=1, xsd=1), gain=f"attn_norm{layer}")
        add("operand", dict(operand=4, feature_turn=4), src="xs", kts=KD, gain=f"attn_norm{layer}")
        if mixer == "A":
            add("qkv", dict(tile=12, slab=6, rope=4, turned=4, split=4, values=2), groups=2)
            add("attend", dict(unit=16, mixes=16, obank=4, xsd=1), mix="A", j=layer // 3)
            add("operand", dict(operand=4, feature_turn=4), src="xs", kts=KD, gain=f"subln{layer // 3}")
            add("out", dict(tile=4, x_ready=1), post=None)
        elif mixer == "B":
            add("latent", dict(tile=3, slab=2))
            add("operand", dict(operand=3, feature_turn=3), src="lat", kts=5, gain="lat")
            add("lift", dict(tile=5, slab=7, values=2))
            for half in range(2):
                add("turn", dict(turned=4, split=4), j=half)
                add("attend", dict(unit=16, obank=4, scaled=16), mix="B", j=half)
            add("operand", dict(operand=4), src="features", kts=KD, gain=None)
            add("out", dict(tile=4, x_ready=1), post=None)
        else:
            for half in range(2):
                add("qkv", dict(tile=18, slab=9, rope=6, turned=6, split=6, values=3), groups=3)
                add("attend", dict(unit=16, obank=4, scaled=16), mix="C", j=half)
            add("operand", dict(operand=4), src="features", kts=KD, gain=None)
            add("out", dict(tile=4, x_ready=1), post=None)
        if layer == LAYERS[-1]:
            add("fetch", dict())
        add("norm", dict(norms=1, xsd=1), gain=f"ffn_norm{layer}")
        add("operand", dict(operand=4, feature_turn=4), src="xs", kts=KD, gain=f"ffn_norm{layer}")
        add("ffn", dict(tile=33, chunk=22, pair=11, x_ready=1), post=None)
    add("final_norm", dict(x_ready=1, rows=1))
    add("norm", dict(norms=1, xsd=1), gain="pre_mix")
    add("operand", dict(operand=4, feature_turn=4), src="xs", kts=KD, gain="pre_mix")
    add("hybrid", dict(tile=9, slab=4, turned=3, split=2, values=1, unit=16, obank=2, operand=2, feature_turn=2), mix="M")
    add("out", dict(tile=4, x_ready=1, rows=1), post="post_mix")
    add("norm", dict(norms=1, xsd=1), gain="pre_ffn")
    add("operand", dict(operand=4, feature_turn=4), src="xs", kts=KD, gain="pre_ffn")
    add("ffn", dict(tile=33, chunk=22, pair=11, x_ready=1, rows=1), post="post_ffn")
    return stages, c["tile"]



SMALL = {}


def _small(name, width):
    SMALL[name] = (sum(w for _, w in SMALL.values()), width)


for _l in range(4):
    _small(f"attn_norm{_l}", KD)
    _small(f"ffn_norm{_l}", KD)
_small("lat", 5)
_small("subln0", 1)
_small("subln1", 1)
_small("pre_mix", KD)
_small("pre_ffn", KD)
_small("ssm_out", 4)
_small("attn_out", 4)
_small("b_glu", 4)
_small("ssm_d", 4)
_small("a_re", 16)
_small("a_im", 16)
_small("log_dt", 16)
SMALL_W = sum(w for _, w in SMALL.values())
CONST = {}


def _const(name, width):
    CONST[name] = (sum(w for _, w in CONST.values()), width)


_const("ident", P)
_const("cos_a", T2 * 16)
_const("sin_a", T2 * 16)
_const("cos_b", T2 * 32)
_const("sin_b", T2 * 32)
_const("mask", 1024)
_const("causal", 384)
_const("ones", P)
CONST_W = sum(w for _, w in CONST.values())


STATES = 64
GROUPS = 32
GIN = 16
STILES = GROUPS * STATES // P
SHIFTS = 8
S5_W = 2 * 4 * P + 2 * STILES * 32


def build_program(nc, x_in, tape, smalls, consts, lam_in, rows_in, s5_in, out):
    stages, tiles = plan()
    hybrid = next(st for st in stages if st.kind == "hybrid")
    with ExitStack() as ctx:
        def sem(name):
            return ctx.enter_context(nc.semaphore(name))

        def psum(name, shape):
            return ctx.enter_context(nc.psum_tensor(name, shape, F32))

        place = {"at": 0}
        room = ctx.enter_context(nc.sbuf_tensor("room", [P, (nc.sbuf_bytes_remaining - 64) // 4], F32))
        base = nc.sbuf_base - room.shape[1] * 4

        def sb(name, shape, dt=F32, at=None):
            size = 4 * int(np.prod(shape[1:]))
            if at is None:
                at = place["at"]
                place["at"] += -(-size // 32) * 32
                assert place["at"] <= room.shape[1] * 4, (name, place["at"])
            return nc.alloc_sbuf_tensor_at(name, shape, dt, offset=base + at)

        raw = sb("raw", [P, RING, TILE])
        w_hi = sb("w_hi", [P, RING, TILE], F32R)
        w_lo = sb("w_lo", [P, RING, TILE], F32R)
        x = sb("x", [P, T2, D])
        xs = sb("xs", [P, T2, D])
        features = xs[:, :, :].rearrange("p t (f n) -> p (t f) n", n=S)
        xT_hi = sb("xT_hi", [P, KD, S], F32R)
        xT_lo = sb("xT_lo", [P, KD, S], F32R)
        small = sb("small", [P, SMALL_W])
        const = sb("const", [P, CONST_W])
        stat = sb("stat", [P, 5, 16])
        sums = sb("sums", [P, 2, 32])
        nmax = sb("nmax", [P, 2, 2])
        lam = sb("lam", [P, 16])
        rot = sb("rot", [P, 2, 256])
        scratch_at = place["at"]
        probs = sb("probs", [P, 2, 768])
        probsT_hi = sb("probsT_hi", [P, 4, 6, P], F32R)
        probsT_lo = sb("probsT_lo", [P, 4, 6, P], F32R)
        hT_hi = sb("hT_hi", [P, 2, 2, S], F32R, at=scratch_at)
        hT_lo = sb("hT_lo", [P, 2, 2, S], F32R, at=scratch_at + 2 * 2 * S * 4)
        stage = sb("stage", [P, 2, T2, BANK], at=scratch_at)
        arena_at = place["at"]
        QT_hi = sb("QT_hi", [P, 12, S], F32R)
        QT_lo = sb("QT_lo", [P, 12, S], F32R)
        KT_hi = sb("KT_hi", [P, 12, S], F32R)
        KT_lo = sb("KT_lo", [P, 12, S], F32R)
        V_hi = sb("V_hi", [P, 3, T2, BANK], F32R)
        V_lo = sb("V_lo", [P, 3, T2, BANK], F32R)
        lam_raw = sb("lam_raw", [P, 768], at=arena_at)
        xT_at = (RING * TILE * 3 + 2 * T2 * D) * 4
        squared = sb("squared", [P, 16, P], at=xT_at)
        h32 = sb("h32", [P, 2, 2, S], at=arena_at)
        sg = sb("sg", [P, 2, S], at=arena_at + 4096)
        q_tm = sb("q_tm", [P, T2, 1536], at=arena_at)
        k_tm = sb("k_tm", [P, T2, 1536], at=arena_at + 12288)
        a_tm = sb("a_tm", [P, T2, 672], at=arena_at + 24576)
        QB_hi = sb("QB_hi", [96, 8, S], F32R, at=arena_at + 24576)
        QB_lo = sb("QB_lo", [96, 8, S], F32R, at=arena_at + 32768)
        KB_hi = sb("KB_hi", [96, 8, S], F32R, at=arena_at + 40960)
        KB_lo = sb("KB_lo", [96, 8, S], F32R, at=arena_at + 49152)
        VB_hi = sb("VB_hi", [P, T2, D], F32R, at=arena_at + 57344)
        VB_lo = sb("VB_lo", [P, T2, D], F32R, at=arena_at + 65536)
        QM_hi, QM_lo, KM_hi, KM_lo = (sb(n, [P, 4, S], F32R, at=arena_at + 4096 * i)
                                      for i, n in enumerate(("QM_hi", "QM_lo", "KM_hi", "KM_lo")))
        VM_hi = sb("VM_hi", [P, 1, T2, BANK], F32R, at=arena_at + 16384)
        VM_lo = sb("VM_lo", [P, 1, T2, BANK], F32R, at=arena_at + 20480)
        y_skip = sb("y_skip", [P, 4, S], at=scratch_at + 6144)
        E_re = sb("E_re", [P, STILES, S], at=arena_at + 24576)
        E_im = sb("E_im", [P, STILES, S], at=arena_at + 40960)
        row = sb("row", [P, D])
        s5 = sb("s5", [P, S5_W], at=arena_at + 57344)
        Cc = sb("Cc", [P, 2, STILES, 32], at=arena_at + 57344 + 4 * S5_W)
        uT = sb("uT", [P, 4, S], at=arena_at + 57344 + 4 * S5_W + 4096)
        B_in = s5[:, 0:1024].rearrange("p (c f n) -> p c f n", c=2, f=4)
        C_in = s5[:, 1024:2048].rearrange("p (c i n) -> p c i n", c=2, i=STILES)
        pre_c = sb("pre_c", [P, 2, S], at=xT_at)
        pre_s = sb("pre_s", [P, 2, S], at=xT_at + 2048)
        scan = sb("scan", [P, 2, 2, S], at=xT_at + 4096)
        post_c = sb("post_c", [P, 2, 2, S], at=xT_at + 8192)
        post_s = sb("post_s", [P, 2, S], at=xT_at + 12288)
        y_act = sb("y_act", [P, 4, S], at=arena_at + 24576)
        sig = sb("sig", [P, 4, S], at=arena_at + 28672)
        y_gated = sb("y_gated", [P, 4, S], at=arena_at + 32768)
        y_sq = sb("y_sq", [P, 4, S], at=arena_at + 36864)
        inv3 = sb("inv3", [P, 3, S], at=arena_at + 40960)
        y_norm = sb("y_norm", [P, 4, S], at=arena_at + 45056)
        h_junk = sb("h_junk", [P, T2, D], at=arena_at + 8192)
        pole = sb("pole", [P, 12, STILES], at=scratch_at + 10240)
        trig = sb("trig", [P, 2, SHIFTS, STILES], at=scratch_at + 11008)
        trig_k = sb("trig_k", [P, 2, SHIFTS, STILES], at=scratch_at + 8192)

        bank = psum("bank", [P, 8, BANK])
        ident = const[:, 0:P]

        def const_ap(name):
            o, w = CONST[name]
            return const[:, o:o + w]

        def gain(name, k):
            return small[:, SMALL[name][0] + k:SMALL[name][0] + k + 1]

        def gains(name):
            o, w = SMALL[name]
            return small[:, o:o + w]

        small_in = sem("small_in")
        x_in_done = sem("x_in_done")
        tape_in = [sem(f"tape_in{i}") for i in range(RING)]
        hi_done = sem("hi_done")
        lo_dve = sem("lo_dve")
        lo_pool = sem("lo_pool")
        w_used = sem("w_used")
        chain = sem("chain")
        inv_ready = sem("inv_ready")
        xs_dve = sem("xs_dve")
        xs_act = sem("xs_act")
        op_turned = sem("op_turned")
        op_hi = sem("op_hi")
        op_lo = sem("op_lo")
        slab_out = sem("slab_out")
        rope_mul = sem("rope_mul")
        rope_done = sem("rope_done")
        turned = sem("turned")
        split_hi = sem("split_hi")
        split_lo = sem("split_lo")
        values_lo = sem("values_lo")
        inputs_out = sem("inputs_out")
        scores = sem("scores")
        maxed = sem("maxed")
        exped = sem("exped")
        mixed = sem("mixed")
        probs_turned = sem("probs_turned")
        pt_hi = sem("pt_hi")
        pt_lo = sem("pt_lo")
        o_done = sem("o_done")
        o_out = sem("o_out")
        o_sq = sem("o_sq")
        inv_sums = sem("inv_sums")
        normed = sem("normed")
        gu_done = sem("gu_done")
        silu_done = sem("silu_done")
        h_done = sem("h_done")
        h_hi = sem("h_hi")
        h_lo = sem("h_lo")
        lam_dots = sem("lam_dots")
        lam_exp = sem("lam_exp")
        sq_act = sem("sq_act")
        x_ready = sem("x_ready")
        lat_ready = sem("lat_ready")
        out_ready = sem("out_ready")
        stored = sem("stored")
        s5_in_done = sem("s5_in_done")
        row_in = sem("row_in")
        row_used = sem("row_used")
        dt_ready = sem("dt_ready")
        pole_ready = sem("pole_ready")
        mag_ready = sem("mag_ready")
        angle_ready = sem("angle_ready")
        trig_ready = sem("trig_ready")
        v_done = sem("v_done")
        v_used = sem("v_used")
        scanned = sem("scanned")
        states = sem("states")
        pool_chain = sem("pool_chain")
        y_done = sem("y_done")
        y_out = sem("y_out")
        gelu_done = sem("gelu_done")
        glu_hi = sem("glu_hi")
        glu_lo = sem("glu_lo")
        sig_done = sem("sig_done")
        sq_done = sem("sq_done")
        ss_done = sem("ss_done")
        norm_done = sem("norm_done")
        mix_hi = sem("mix_hi")
        mix_lo = sem("mix_lo")
        hybrid_xs = sem("hybrid_xs")

        block = ctx.enter_context(nc.Block())

        def lo_part(eng, at, lo, hi):
            eng.wait_ge(hi_done, at.count + 1)
            return eng.tensor_tensor(w_lo[:, at.slot, lo:hi], raw[:, at.slot, lo:hi],
                                     w_hi[:, at.slot, lo:hi].bitcast(F32), ALU.subtract)

        def unit_list(st):
            return [(h, t) for h in range(8) for t in range(T2)]

        def turn_banks(st, u):
            return (4, 5) if st.mix == "C" else (4,) if st.mix == "M" else (4 + u % 2,)

        def by_feature(st):
            return st.mix in "BC"

        def turned_buffer(st, u):
            return u % 4 if by_feature(st) else 2 + u % 2

        def buffer_free(st, u):
            if by_feature(st):
                return st.unit + (u // 2 - 1) * 2 if u >= 4 else None
            return st.unit + u - 1 if u >= 2 else None

        def key_block(st, t, k):
            return group_order(st, t)[k // 2] * 2 + k % 2 if st.mix == "C" else k

        def group_order(st, t):
            if st.mix == "C":
                return (0, 1, 2) if t == 0 else (1, 2, 0)
            return (0,)

        def operands(mix):
            if mix == "B":
                return (QB_hi, QB_lo), (KB_hi, KB_lo), (VB_hi, VB_lo)
            if mix == "M":
                return (QM_hi, QM_lo), (KM_hi, KM_lo), (VM_hi, VM_lo)
            return (QT_hi, QT_lo), (KT_hi, KT_lo), (V_hi, V_lo)

        def block_part(x, b, n):
            return x[:, b * n:(b + 1) * n] if type(b) is int else x[:, bass.ds(b * n, n)]

        @block.sync
        def _(sp):
            sp.dma_start(x[:], x_in.rearrange("(t p) d -> p t d", p=P)).then_inc(x_in_done, 16)
            sp.dma_start(const[:], consts).then_inc(small_in, 16)
            sp.dma_start(small[:], smalls).then_inc(small_in, 16)
            sp.dma_start(lam_raw[:, 0:512], lam_in.partition_broadcast(P)).then_inc(small_in, 16)
            for n in range(RING):
                sp.dma_start(raw[:, n, :], tape[n]).then_inc(tape_in[n], 16)

            def load(at):
                sp.wait_ge(lo_dve, at.count - RING + 1)
                sp.wait_ge(lo_pool, at.count - RING + 1)
                sp.dma_start(raw[:, at.slot, :], tape[bass.ds(at.count, 1), :, :].rearrange("a p n -> (a p) n")
                             ).then_inc(tape_in[at.slot], 16)

            turns = tiles // RING
            with sp.Fori(1, turns) as turn:
                for slot in range(RING):
                    load(Place(slot, turn))
            for n in range(turns * RING, tiles):
                load(Place(n))
            sp.wait_ge(out_ready, 1)
            sp.dma_start(out.rearrange("(t p) d -> p t d", p=P), x[:]).then_inc(stored, 16)
            sp.wait_ge(stored, 16)

        @block.gpsimd
        def _(pool):
            def low_parts(first, end):
                a = min(-(-first // RING) * RING, end)
                b = max(end // RING * RING, a)
                for n in range(first, a):
                    lo_part(pool, Place(n), SPLIT_DVE, TILE).then_inc(lo_pool, 1)
                if b > a:
                    with pool.Fori(a // RING, b // RING) as turn:
                        for slot in range(RING):
                            lo_part(pool, Place(slot, turn), SPLIT_DVE, TILE).then_inc(lo_pool, 1)
                for n in range(b, end):
                    lo_part(pool, Place(n), SPLIT_DVE, TILE).then_inc(lo_pool, 1)

            def link(ins, links):
                links[0] += 1
                ins.then_inc(pool_chain, 1)
                pool.wait_ge(pool_chain, links[0])

            def rotate_back(links):
                for i in range(STILES):
                    er = E_re[:, i, :].unsqueeze(1).broadcast_to([P, 2, S])
                    ei = E_im[:, i, :].unsqueeze(1).broadcast_to([P, 2, S])
                    pc = post_c[:, i % 2, :, :]
                    pool.wait_ge(scanned, i + 1)
                    if i >= 2:
                        pool.wait_ge(y_done, i - 1)
                    if i >= 1:
                        pool.wait_ge(states, i)
                    pool.tensor_tensor(pc, scan[:, i % 2, :, :], er, ALU.mult)
                    link(pool.tensor_tensor(post_s[:, :, :], scan[:, i % 2, :, :], ei, ALU.mult), links)
                    pool.tensor_tensor(pc[:, 0, :], pc[:, 0, :], post_s[:, 1, :], ALU.subtract)
                    pool.tensor_tensor(pc[:, 1, :], pc[:, 1, :], post_s[:, 0, :], ALU.add).then_inc(states, 1)

            stop = hybrid.tile + 8 + LEAD
            low_parts(0, stop)
            rotate_back([0])
            low_parts(stop, tiles)

        @block.tensor
        def _(pe):
            def weights(at):
                pe.wait_ge(lo_dve, at.count + 1)
                pe.wait_ge(lo_pool, at.count + 1)

            def product(o, l_hi, l_lo, r_hi, r_lo, start, stop):
                pe.matmul(o, l_hi, r_hi, start=start, stop=False)
                pe.matmul(o, l_hi, r_lo, start=False, stop=False)
                return pe.matmul(o, l_lo, r_hi, start=False, stop=stop)

            def operand_ready(st):
                pe.wait_ge(op_lo, st.operand)

            def operand(st):
                if st.src == "features":
                    return
                if st.src == "xs":
                    pe.wait_ge(xs_dve, st.xsd)
                    pe.wait_ge(xs_act, st.norms)
                    if st.obank:
                        pe.wait_ge(o_out, st.obank)
                else:
                    pe.wait_ge(lat_ready, 1)
                if st.operand == 0:
                    pe.wait_ge(small_in, 48)
                for b in range(-(-st.kts // 2)):
                    ks = range(2 * b, min(2 * b + 2, st.kts))
                    for k in ks:
                        for t in range(T2):
                            src = (xs if st.src == "xs" else a_tm)[:, t, k * P:(k + 1) * P]
                            o = (k % 2) * S + t * P
                            last = pe.transpose(bank[:, 4 + b, o:o + P], src, ident)
                    last.then_inc(op_turned, 1)

            def qkv_slab(at, s_count, pair, check):
                if check:
                    pe.wait_ge(slab_out, s_count - 2)
                for half in range(2):
                    weights(at + half)
                    for kk in range(4):
                        k = half * 4 + kk
                        for t in range(T2):
                            sl = (at + half).slot
                            last = product(bank[:, 2 * pair + t, :],
                                           xT_hi[:, k, t * P:(t + 1) * P], xT_lo[:, k, t * P:(t + 1) * P],
                                           w_hi[:, sl, kk * BANK:(kk + 1) * BANK],
                                           w_lo[:, sl, kk * BANK:(kk + 1) * BANK],
                                           start=(k == 0), stop=(k == KD - 1))
                    last.then_inc(w_used, 1)

            def turn_slab(buf, split, check):
                if check:
                    pe.wait_ge(split_lo, split)
                for ft in range(4):
                    for t in range(T2):
                        b, o = divmod(ft * S + t * P, BANK)
                        last = pe.transpose(bank[:, 6 + b, o:o + P], stage[:, buf, t, ft * P:(ft + 1) * P], ident)
                last.then_inc(turned, 1)

            def qkv_block(at, s0, r0, split, values, check, rope=True):
                qkv_slab(at, s0, 0, check)
                qkv_slab(at + 2, s0 + 1, 1, check)
                pe.wait_ge(rope_done if rope else slab_out, (r0 if rope else s0) + 1)
                turn_slab(0, split, check)
                if check:
                    pe.wait_ge(values_lo, values)
                qkv_slab(at + 4, s0 + 2, 2, check)
                pe.wait_ge(rope_done if rope else slab_out, (r0 if rope else s0) + 2)
                turn_slab(1, split + 1, True)

            def qkv(st):
                operand_ready(st)
                if st.slab == 0:
                    for b in range(st.groups):
                        qkv_block(Place(st.tile + 6 * b), st.slab + 3 * b, st.rope + 2 * b, st.split + 2 * b,
                                  st.values + b, b > 0)
                else:
                    with pe.Fori(0, st.groups) as b:
                        qkv_block(Place(st.tile, b * 2), b * 3 + st.slab, b * 2 + st.rope, b * 2 + st.split,
                                  b + st.values, True)

            def latent(st):
                operand_ready(st)
                qkv_slab(Place(st.tile), st.slab, 0, True)
                at = Place(st.tile + 2)
                weights(at)
                for t in range(T2):
                    for k in range(KD):
                        last = product(bank[:, 2 + t, 0:160], xT_hi[:, k, t * P:(t + 1) * P],
                                       xT_lo[:, k, t * P:(t + 1) * P], w_hi[:, at.slot, k * 160:(k + 1) * 160],
                                       w_lo[:, at.slot, k * 160:(k + 1) * 160], start=(k == 0), stop=(k == KD - 1))
                last.then_inc(w_used, 1)

            def lift(st):
                operand_ready(st)
                s = st.slab
                for i in range(7):
                    at, lo, kts, k0 = (Place(st.tile + i), 0, 3, 0) if i < 3 else \
                        (Place(st.tile + 3 + (i - 3) // 2), ((i - 3) % 2) * BANK, 2, 3)
                    width = BANK if i < 3 else 2 * BANK
                    pe.wait_ge(slab_out, s + i - 2)
                    weights(at)
                    for k in range(kts):
                        for t in range(T2):
                            c = k * width + lo
                            last = product(bank[:, 2 * (i % 3) + t, :], xT_hi[:, k0 + k, t * P:(t + 1) * P],
                                           xT_lo[:, k0 + k, t * P:(t + 1) * P], w_hi[:, at.slot, c:c + BANK],
                                           w_lo[:, at.slot, c:c + BANK], start=(k == 0), stop=(k == kts - 1))
                    if i < 3 or i % 2 == 0:
                        last.then_inc(w_used, 1)

            def turn_heads(st):
                pe.wait_ge(lat_ready, 3)
                pe.wait_ge(slab_out, st.slab)
                pe.wait_ge(values_lo, st.values)
                pe.wait_ge(o_out, st.obank)
                for i in range(4):
                    pe.wait_ge(split_lo, st.split + i - 1)
                    src = q_tm if i < 2 else k_tm
                    for hh in range(4):
                        for t in range(T2):
                            h = st.j * 8 + (i % 2) * 4 + hh
                            b, o = divmod(hh * S + t * P, BANK)
                            last = pe.transpose(bank[0:96, 4 + 2 * (i % 2) + b, o:o + P],
                                                src[:, t, h * 96:(h + 1) * 96], ident)
                    last.then_inc(turned, 1)

            def attend(st, beside=lambda u: None):
                units = unit_list(st)
                U = st.unit
                pe.wait_ge(split_lo, st.split + (2 if st.mix == "M" else 0))
                pe.wait_ge(values_lo, st.values + (1 if st.mix == "M" else 0))
                q, k_, v_ = operands(st.mix)

                def score(u):
                    h, t = units[u]
                    if u >= 2:
                        pe.wait_ge(maxed if st.mix in "CM" else exped, U + u - 1)
                    b = 2 * (u % 2)
                    qs = slice(t * P, (t + 1) * P)
                    if st.mix == "A":
                        for sub in range(2):
                            r = slice(sub * 64, sub * 64 + 64)
                            last = product(bank[:, b + sub, 0:S], q[0][r, h, qs], q[1][r, h, qs], k_[0][r, h, :],
                                           k_[1][r, h, :], start=True, stop=True)
                    elif st.mix == "B":
                        last = product(bank[:, b, 0:S], q[0][:, h, qs], q[1][:, h, qs], k_[0][:, h, :],
                                       k_[1][:, h, :], start=True, stop=True)
                    else:
                        r = slice((h % 2) * 64, (h % 2) * 64 + 64)
                        for i, g in enumerate(group_order(st, t)):
                            f = g * 4 + h // 2
                            bb, o = divmod(i * S, BANK)
                            last = product(bank[:, b + bb, o:o + S], q[0][r, f, qs], q[1][r, f, qs],
                                           k_[0][r, f, :], k_[1][r, f, :], start=True, stop=True)
                    last.then_inc(scores, 1)

                def transposed(u):
                    pe.wait_ge(pt_lo, U + u + 1)

                def turn(u):
                    if by_feature(st):
                        pe.wait_ge(normed, st.scaled + u + 1)
                    elif st.mix == "A":
                        pe.wait_ge(mixed, st.mixes + u + 1)
                    else:
                        pe.wait_ge(exped, U + u + 1)
                    if u >= (1 if st.mix in "CM" else 2):
                        transposed(u - (1 if st.mix in "CM" else 2))
                    banks = turn_banks(st, u)
                    n = 6 if st.mix == "C" else 2
                    for k in range(n):
                        b, o = divmod(key_block(st, units[u][1], k) * P, BANK)
                        last = pe.transpose(bank[:, banks[b], o:o + P], probs[:, u % 2, k * P:(k + 1) * P], ident)
                    last.then_inc(probs_turned, 1)

                def weigh(u):
                    h, t = units[u]
                    d = 128 if st.mix == "A" else 64
                    per = BANK // d
                    o_banks = 1 if st.mix == "M" else 2
                    if u % per == 0 and u // per >= o_banks:
                        pe.wait_ge(o_out, st.obank + u // per - o_banks + 1)
                    transposed(u)
                    o = bank[:, 6 + (u // per) % o_banks, (u % per) * d:(u % per + 1) * d]
                    n = 6 if st.mix == "C" else 2
                    order = group_order(st, t)
                    for k in range(n):
                        if st.mix == "A":
                            g, c = h // 4, (h % 4) * d
                        elif st.mix == "B":
                            g, c = None, (st.j * 8 + h) * d
                        else:
                            g, c = order[k // 2], h * d
                        v = [x[:, k % 2, c:c + d] if g is None else x[:, g, k % 2, c:c + d] for x in v_]
                        tb = turned_buffer(st, u)
                        last = product(o, probsT_hi[:, tb, k, :], probsT_lo[:, tb, k, :], v[0], v[1],
                                       start=(k == 0), stop=(k == n - 1))
                    last.then_inc(o_done, 1)

                def weigh_head(h, first, end):
                    if h >= 4 and first == 0:
                        pe.wait_ge(o_out, st.obank + 2)
                    transposed(2 * h + 1)
                    tb = (2 * h) % 4
                    o = bank[0:64, 6 + h % 2, (h // 2 % 2) * S:(h // 2 % 2 + 1) * S].rearrange("p (t n) -> p t n", n=P)
                    blocks_ = 6 if st.mix == "C" else 2
                    c = h * 64 if st.mix == "C" else (st.j * 8 + h) * 64
                    for k in range(first, end):
                        v = [y[:, k // 2, k % 2, c:c + 64] if st.mix == "C" else y[:, k, c:c + 64] for y in v_]
                        p_hi, p_lo = probsT_hi[:, tb:tb + 2, k, :], probsT_lo[:, tb:tb + 2, k, :]
                        pe.matmul(o, v[0], p_hi, start=(k == 0), stop=False)
                        before = pe.matmul(o, v[0], p_lo, start=False, stop=False)
                        last = pe.matmul(o, v[1], p_hi, start=False, stop=(k == blocks_ - 1))
                    if end == blocks_:
                        before.then_inc(o_done, 1)
                        last.then_inc(o_done, 1)

                n = len(units)
                score(0)
                score(1)
                if by_feature(st):
                    half_blocks = 3 if st.mix == "C" else 1
                    for u in range(n + 2):
                        if u < n:
                            turn(u)
                        if u + 2 < n:
                            score(u + 2)
                        if u >= 2:
                            part = u % 2
                            weigh_head((u - 2) // 2, part * half_blocks, (part + 1) * half_blocks)
                    return
                behind = 2 if st.mix == "A" else 1
                for u in range(n + behind):
                    if u < n:
                        turn(u)
                    if u + 2 < n:
                        score(u + 2)
                    if u >= behind:
                        weigh(u - behind)
                    beside(u)

            def acc_tile(at, k0, l_hi, l_lo, start, stop):
                weights(at)
                for kk in range(2):
                    for t in range(T2):
                        for half in range(2):
                            c = kk * D + half * BANK
                            last = product(bank[:, 2 * t + half, :], l_hi[:, k0 + kk, t * P:(t + 1) * P],
                                           l_lo[:, k0 + kk, t * P:(t + 1) * P],
                                           w_hi[:, at.slot, c:c + BANK], w_lo[:, at.slot, c:c + BANK],
                                           start=start and kk == 0, stop=stop and kk == 1)
                last.then_inc(w_used, 1)

            def hybrid_layer(st):
                operand_ready(st)
                at = Place(st.tile)

                qkv_slab(at, st.slab, 2, True)
                pe.wait_ge(slab_out, st.slab + 1)
                turn_slab(1, st.split, True)
                pe.wait_ge(inputs_out, 1)
                qkv_block(at + 2, st.slab + 1, None, st.split, st.values, True, rope=False)

                def drive(i):
                    if i >= 2:
                        pe.wait_ge(v_used, i - 1)
                    p0 = (i % 4) * 32
                    for c in range(2):
                        last = pe.matmul(bank[:, 1 + 2 * (i % 2), c * S:(c + 1) * S], B_in[p0:p0 + 32, c, i // 4, :],
                                         uT[p0:p0 + 32, i // 4, :], start=True, stop=True)
                    last.then_inc(v_done, 1)

                def read_out(i):
                    pe.wait_ge(states, i + 1)
                    if i % 4 == 0 and i >= 8:
                        pe.wait_ge(y_out, i // 4 - 1)
                    p0 = (i % 4) * 32
                    o = bank[p0:p0 + 32, 5 + 2 * ((i // 4) % 2), 0:S]
                    for c in range(2):
                        last = pe.matmul(o, Cc[:, c, i, :], post_c[:, i % 2, c, :], start=(c == 0), stop=(c == 1))
                    last.then_inc(y_done, 1)

                def beside(u):
                    if u < STILES:
                        drive(u)
                    if u >= 2:
                        read_out(u - 2)

                pe.wait_ge(s5_in_done, 16)
                pe.wait_ge(pole_ready, 1)
                attend(st, beside)
                read_out(STILES - 1)
                pe.wait_ge(glu_hi, 1)
                pe.wait_ge(glu_lo, 1)
                weights(at + 8)
                sl = (at + 8).slot
                for e in range(4):
                    b = bank[:, e // 2, (e % 2) * S:(e % 2 + 1) * S]
                    for k in range(4):
                        w = slice(k * BANK + e * P, k * BANK + (e + 1) * P)
                        pe.matmul(b, w_hi[:, sl, w], xT_hi[:, k, :], start=(k == 0), stop=False)
                        pe.matmul(b, w_hi[:, sl, w], xT_lo[:, k, :], start=False, stop=False)
                        last = pe.matmul(b, w_lo[:, sl, w], xT_hi[:, k, :], start=False, stop=(k == 3))
                last.then_inc(w_used, 1)
                pe.wait_ge(hybrid_xs, 1)
                for k in range(4):
                    for t in range(T2):
                        o = (k % 2) * S + t * P
                        last = pe.transpose(bank[:, 4 + k // 2, o:o + P], xs[:, t, k * P:(k + 1) * P], ident)
                    if k % 2:
                        last.then_inc(op_turned, 1)
                pe.wait_ge(sq_done, 1)
                for k in range(4):
                    last = pe.matmul(bank[:, 2, 0:S], const_ap("ones"), y_sq[:, k, :], start=(k == 0), stop=(k == 3))
                last.then_inc(ss_done, 1)

            def out_projection(st):
                operand_ready(st)
                if st.post == "post_mix":
                    pe.wait_ge(mix_lo, 1)
                for i in range(4):
                    acc_tile(Place(st.tile + i), 2 * i, xT_hi, xT_lo, i == 0, i == 3)

            def ffn(st):
                operand_ready(st)
                C, J = st.chunk, st.pair

                def hidden(at, c, c_mod, check):
                    if check:
                        pe.wait_ge(h_done, c - 3)
                    weights(at)
                    for part in range(2):
                        for k in range(KD):
                            o = k * 2 * P + part * P
                            w = slice(o, o + P)
                            b = bank[:, 4 + c_mod, part * S:(part + 1) * S]
                            pe.matmul(b, w_hi[:, at.slot, w], xT_hi[:, k, :], start=(k == 0), stop=False)
                            pe.matmul(b, w_hi[:, at.slot, w], xT_lo[:, k, :], start=False, stop=False)
                            last = pe.matmul(b, w_lo[:, at.slot, w], xT_hi[:, k, :], start=False, stop=(k == KD - 1))
                    last.then_inc(w_used, 1)

                def down(at, j, buf, start, stop):
                    pe.wait_ge(h_lo, j + 1)
                    acc_tile(at, 0, hT_hi[:, buf, :, :], hT_lo[:, buf, :, :], start, stop)

                def pair(at, c, j, p, first, check):
                    hidden(at, c, (2 * p) % 4, check)
                    hidden(at + 1, c + 1, (2 * p + 1) % 4, check)
                    down(at + 2, j - 1, (p + 1) % 2, first, False)

                at = Place(st.tile)
                hidden(at, C, 0, False)
                hidden(at + 1, C + 1, 1, False)
                pair(at + 2, C + 2, J + 1, 1, True, False)
                pair(at + 5, C + 4, J + 2, 0, False, True)
                with pe.Fori(0, 3) as i:
                    for p in range(2):
                        pair(Place(st.tile + 8 + 3 * p, i * 2), i * 4 + (C + 6 + 2 * p), i * 2 + (J + 3 + p),
                             (1 + p) % 2, False, True)
                for p in range(2):
                    pair(at + 26 + 3 * p, C + 18 + 2 * p, J + 9 + p, (1 + p) % 2, False, True)
                down(at + 32, J + 10, 0, False, True)

            pe.sem_inc(w_used, RING)
            for st in stages:
                {"operand": operand, "qkv": qkv, "latent": latent, "lift": lift, "turn": turn_heads, "attend": attend,
                 "out": out_projection, "ffn": ffn, "norm": lambda s: None, "final_norm": lambda s: None,
                 "fetch": lambda s: None, "hybrid": hybrid_layer}[st.kind](st)


        @block.scalar
        def _(act):
            def hi_part(at):
                if type(at.count) is int and at.count >= tiles:
                    return
                act.wait_ge(tape_in[at.slot], at.round * 16 + 16)
                act.wait_ge(w_used, at.count + 1)
                act.activation(w_hi[:, at.slot, :], raw[:, at.slot, :], ACT.Copy).then_inc(hi_done, 1)

            def tile_done(at):
                act.wait_ge(w_used, at.count + RING + 1)

            def norm(st):
                act.wait_ge(x_in_done if st.norms == 0 else x_ready, 16 if st.norms == 0 else st.x_ready)
                act.activation(xs[:, 1, :], x[:, 1, :], ACT.Square, accum_out=stat[:, 0, 1:2]).then_inc(sq_act, 1)
                act.wait_ge(inv_ready, st.norms + 1)
                act.activation(xs[:, 1, :], x[:, 1, :], ACT.Copy, scale=stat[:, 2, 1:2]).then_inc(xs_act, 1)

            def operand(st):
                if st.src == "features":
                    act.wait_ge(o_out, st.obank)
                    for b in range(4):
                        act.activation(xT_hi[:, 2 * b:2 * b + 2, :], features[:, 2 * b:2 * b + 2, :], ACT.Copy
                                       ).then_inc(op_hi, 1)
                    return
                for b in range(-(-st.kts // 2)):
                    act.wait_ge(op_turned, st.feature_turn + b + 1)
                    for k in range(2 * b, min(2 * b + 2, st.kts)):
                        src = bank[:, 4 + b, (k % 2) * S:(k % 2 + 1) * S]
                        g = 1.0 if st.gain is None else gain(st.gain, 0 if "subln" in st.gain else k)
                        last = act.activation(xT_hi[:, k, :], src, ACT.Copy, scale=g)
                    last.then_inc(op_hi, 1)

            def turned_high(dst, b, t, first_bank=6, parts=P):
                act.wait_ge(turned, t)
                src = bank[0:parts, first_bank:first_bank + 2, :].rearrange("p b n -> p (b n)")
                act.activation(block_part(dst, b, 4), src.rearrange("p (f n) -> p f n", n=S), ACT.Copy
                               ).then_inc(split_hi, 1)

            def qkv_block(at, s0, t0, b, check, parts, scale_q=0.125):
                q, k, v = parts
                for s in range(3):
                    hi_part(at + (2 * s + LEAD))
                    hi_part(at + (2 * s + LEAD + 1))
                    tile_done(at + (2 * s + 1))
                    src = bank[:, 2 * s:2 * s + 2, :]
                    if s < 2:
                        if check:
                            act.wait_ge(turned, t0 + (s - 1))
                        act.activation(stage[:, s, :, :], src, ACT.Copy,
                                       scale=scale_q if s == 0 else 1.0).then_inc(slab_out, 1)
                    else:
                        act.activation(block_part(v[0], b, 1).rearrange("p a t n -> p (a t) n"), src, ACT.Copy
                                       ).then_inc(slab_out, 1)
                    if s >= 1:
                        turned_high((q, k)[s - 1][0], b, t0 + s)

            def qkv(st):
                parts = operands("A")
                if st.slab == 0:
                    for b in range(st.groups):
                        qkv_block(Place(st.tile + 6 * b), st.slab + 3 * b, st.turned + 2 * b, b, b > 0, parts)
                else:
                    with act.Fori(0, st.groups) as b:
                        qkv_block(Place(st.tile, b * 2), b * 3 + st.slab, b * 2 + st.turned, b, True, parts)

            def turn_heads(st):
                for i in range(4):
                    turned_high((QB_hi, KB_hi)[i // 2], i % 2, st.turned + i + 1, 4 + 2 * (i % 2), 96)

            def latent(st):
                at = Place(st.tile)
                hi_part(at + 2)
                hi_part(at + 3)
                tile_done(at + 1)
                act.activation(a_tm[:, :, 0:BANK], bank[:, 0:2, :], ACT.Copy).then_inc(slab_out, 1)
                hi_part(at + 4)
                tile_done(at + 2)
                act.activation(a_tm[:, :, BANK:672], bank[:, 2:4, 0:160], ACT.Copy).then_inc(slab_out, 1)

            def lift(st):
                at = Place(st.tile)
                k4 = k_tm[:, :, :].rearrange("p t (h d) -> p t h d", d=96)
                for i in range(7):
                    tile = at + (i if i < 3 else 3 + (i - 3) // 2)
                    if i < 3 or i % 2 == 1:
                        hi_part(tile + LEAD)
                    tile_done(tile)
                    src = bank[:, 2 * (i % 3):2 * (i % 3) + 2, :]
                    if i < 3:
                        act.activation(q_tm[:, :, i * BANK:(i + 1) * BANK], src, ACT.Copy,
                                       scale=float(np.float32(96.0) ** np.float32(-0.5))).then_inc(slab_out, 1)
                    elif i < 5:
                        for t in range(T2):
                            last = act.activation(k4[:, t, (i - 3) * 8:(i - 2) * 8, 0:64],
                                                  src[:, t, :].rearrange("p (h d) -> p h d", d=64), ACT.Copy)
                        last.then_inc(slab_out, 1)
                    else:
                        act.activation(VB_hi[:, :, (i - 5) * BANK:(i - 4) * BANK], src, ACT.Copy).then_inc(slab_out, 1)

            def attend(st):
                units = unit_list(st)
                n, U = len(units), st.unit

                def expo(u):
                    if u >= 2:
                        act.wait_ge(probs_turned, U + u - 1)
                    act.wait_ge(maxed, U + u + 1)
                    if st.mix == "A":
                        for sub in range(2):
                            last = act.activation(probs[:, u % 2, sub * S:(sub + 1) * S],
                                                  bank[:, 2 * (u % 2) + sub, 0:S], ACT.Exp,
                                                  bias=nmax[:, u % 2, sub:sub + 1], accum_out=sums[:, sub, u:u + 1])
                    else:
                        w = 768 if st.mix == "C" else S
                        src = bank[:, 2 * (u % 2), 0:S] if st.mix == "B" else probs[:, u % 2, 0:w]
                        last = act.activation(probs[:, u % 2, 0:w], src, ACT.Exp, bias=nmax[:, u % 2, 0:1],
                                              accum_out=sums[:, 0, u:u + 1])
                    last.then_inc(exped, 1)

                def copy_turned(u):
                    act.wait_ge(probs_turned, U + u + 1)
                    free = buffer_free(st, u)
                    if free is not None:
                        act.wait_ge(o_done, free)
                    tb = turned_buffer(st, u)
                    n_ = 6 if st.mix == "C" else 2
                    b = turn_banks(st, u)[0]
                    src = bank[:, b:b + 2, :].rearrange("p b n -> p (b n)")[:, 0:n_ * P] if n_ > 4 \
                        else bank[:, b, 0:n_ * P]
                    act.activation(probsT_hi[:, tb, 0:n_, :], src.rearrange("p (k q) -> p k q", q=P), ACT.Copy
                                   ).then_inc(pt_hi, 1)

                def squares(b):
                    act.wait_ge(o_out, st.obank + b + 1)
                    for u in range(4 * b, 4 * b + 4):
                        h, t = units[u]
                        last = act.activation(squared[:, u, :], xs[:, t, h * P:(h + 1) * P], ACT.Square,
                                              accum_out=stat[:, 0, t * 8 + h:t * 8 + h + 1])
                    last.then_inc(o_sq, 1)

                def normalize(u):
                    w = 768 if st.mix == "C" else S
                    act.wait_ge(inv_sums, st.scaled + u + 1)
                    act.activation(probs[:, u % 2, 0:w], probs[:, u % 2, 0:w], ACT.Copy, scale=sums[:, 1, u:u + 1]
                                   ).then_inc(normed, 1)

                expo(0)
                if by_feature(st):
                    for u in range(n + 1):
                        if u < n:
                            normalize(u)
                        if u >= 1:
                            copy_turned(u - 1)
                        if u + 1 < n:
                            expo(u + 1)
                    return
                if st.mix == "A":
                    for u in range(n + 1):
                        if u >= 1:
                            copy_turned(u - 1)
                        if u + 1 < n:
                            expo(u + 1)
                        if u % 4 == 3 and u >= 7:
                            squares(u // 4 - 1)
                    squares(3)
                    return
                for u in range(n):
                    if u + 1 < n:
                        expo(u + 1)
                    copy_turned(u)

            def fetch(st):
                act.wait_ge(x_ready, st.x_ready)
                act.dma_start(s5[:], s5_in).then_inc(s5_in_done, 16)
                act.dma_start(row[:], rows_in[0].partition_broadcast(P)).then_inc(row_in, 16)

            def fetch_row(n):
                act.wait_ge(row_used, n)
                act.dma_start(row[:], rows_in[n].partition_broadcast(P)).then_inc(row_in, 16)

            def hybrid_layer(st):
                at = Place(st.tile)
                fetch_row(1)
                act.activation(pole[:, 0, :], gains("log_dt"), ACT.Exp).then_inc(dt_ready, 1)
                act.wait_ge(mag_ready, 1)
                act.activation(pole[:, 2, :], pole[:, 1, :], ACT.Exp).then_inc(dt_ready, 1)
                act.wait_ge(angle_ready, 1)
                act.activation(trig_k[:, :, :, :], trig[:, :, :, :], ACT.Sin, scale=6.2831853).then_inc(trig_ready, 1)
                hi_part(at + LEAD)
                hi_part(at + (LEAD + 1))
                tile_done(at + 1)
                act.activation(stage[:, 1, :, :], bank[:, 4:6, :], ACT.Copy).then_inc(slab_out, 1)
                act.wait_ge(turned, st.turned + 1)
                act.activation(uT[:, :, :], bank[:, 6:8, :].rearrange("p b n -> p (b n)").rearrange(
                    "p (f n) -> p f n", n=S), ACT.Copy).then_inc(inputs_out, 1)
                qkv_block(at + 2, st.slab + 1, st.turned + 1, 0, True, operands("M"))
                attend(st)
                act.wait_ge(y_out, 4)
                act.activation(y_act[:, :, :], y_skip[:, :, :], ACT.Gelu_apprx_tanh).then_inc(gelu_done, 1)
                act.wait_ge(gelu_done, 1)
                act.activation(xT_hi[:, 0:4, :], y_act[:, :, :], ACT.Copy).then_inc(glu_hi, 1)
                hi_part(at + (8 + LEAD))
                tile_done(at + 8)
                for e in range(4):
                    last = act.activation(sig[:, e, :], bank[:, e // 2, (e % 2) * S:(e % 2 + 1) * S], ACT.Sigmoid,
                                          bias=gain("b_glu", e))
                last.then_inc(sig_done, 1)
                for b in range(2):
                    act.wait_ge(op_turned, st.feature_turn + b + 1)
                    for k in (2 * b, 2 * b + 1):
                        last = act.activation(xT_hi[:, 4 + k, :], bank[:, 4 + b, (k % 2) * S:(k % 2 + 1) * S], ACT.Copy,
                                              scale=gain("attn_out", k))
                    last.then_inc(op_hi, 1)
                act.wait_ge(norm_done, 1)
                for k in range(4):
                    last = act.activation(xT_hi[:, k, :], y_norm[:, k, :], ACT.Copy, scale=gain("ssm_out", k))
                last.then_inc(mix_hi, 1)

            def out_projection(st):
                for i in range(4):
                    hi_part(Place(st.tile + i + LEAD))
                if st.post:
                    fetch_row(2)

            def ffn(st):
                C, J = st.chunk, st.pair

                def silu(at, c, c_mod, check):
                    tile_done(at)
                    if check:
                        act.wait_ge(h_done, c - 1)
                    act.activation(sg[:, c_mod % 2, :], bank[:, 4 + c_mod, 0:S], ACT.Silu).then_inc(silu_done, 1)

                def h_high(c, buf):
                    act.wait_ge(h_done, c + 2)
                    act.activation(hT_hi[:, buf, :, :], h32[:, buf, :, :], ACT.Copy).then_inc(h_hi, 1)

                def pair(at, c, p, check=True):
                    hi_part(at + LEAD)
                    silu(at, c, 2 * p, check)
                    hi_part(at + (LEAD + 1))
                    silu(at + 1, c + 1, 2 * p + 1, check)
                    if check:
                        hi_part(at + (LEAD + 2))
                    h_high(c, p)

                at = Place(st.tile)
                pair(at, C, 0, False)
                pair(at + 2, C + 2, 1)
                pair(at + 5, C + 4, 0)
                with act.Fori(0, 3) as i:
                    for p in range(2):
                        pair(Place(st.tile + 8 + 3 * p, i * 2), i * 4 + (C + 6 + 2 * p), (1 + p) % 2)
                for p in range(2):
                    pair(at + (26 + 3 * p), C + 18 + 2 * p, (1 + p) % 2)
                hi_part(at + (32 + LEAD))

            for n in range(LEAD):
                hi_part(Place(n))
            act.wait_ge(lam_dots, 1)
            act.activation(lam[:, 8:12], lam[:, 4:8], ACT.Exp).then_inc(lam_exp, 1)
            for st in stages:
                {"operand": operand, "qkv": qkv, "latent": latent, "lift": lift, "turn": turn_heads,
                 "attend": attend, "out": out_projection, "ffn": ffn, "norm": norm, "fetch": fetch, "final_norm": lambda s: None,
                 "hybrid": hybrid_layer}[st.kind](st)

        @block.vector
        def _(dve):
            links = [0]

            def link(ins):
                links[0] += 1
                ins.then_inc(chain, 1)
                dve.wait_ge(chain, links[0])

            def lo(at):
                if type(at.count) is int and at.count >= tiles:
                    return
                lo_part(dve, at, 0, SPLIT_DVE).then_inc(lo_dve, 1)

            def rsqrt(n, at=None):
                at = stat[:, 1:4, 0:n] if at is None else at
                v, y, a = at[:, 0, :], at[:, 1, :], at[:, 2, :]
                link(dve.tensor_scalar(a.bitcast(I32), v.bitcast(I32), 1, None, ALU.logical_shift_right))
                link(dve.tensor_scalar(y.bitcast(I32), a.bitcast(I32), -1.0, float(0x5F3759DF), ALU.mult, ALU.add))
                for step in range(3):
                    link(dve.scalar_tensor_tensor(a, y, -0.5, y, ALU.mult, ALU.mult))
                    link(dve.tensor_tensor(a, a, v, ALU.mult))
                    last = dve.scalar_tensor_tensor(y, a, 1.5, y, ALU.add, ALU.mult)
                    if step < 2:
                        link(last)
                return last

            def square_sum(src, width, col, junk):
                return dve.tensor_tensor_reduce(out=junk, in0=src, in1=src, scale=1.0, scalar=0.0, op0=ALU.mult,
                                                op1=ALU.add, accum_out=stat[:, 0, col:col + 1])

            def norm(st):
                if st.norms == 0:
                    dve.wait_ge(x_in_done, 16)
                link(square_sum(x[:, 0, :], D, 0, xs[:, 0, :]))
                dve.wait_ge(sq_act, st.norms + 1)
                link(dve.tensor_scalar(stat[:, 1, 0:2], stat[:, 0, 0:2], 1.0 / D, EPS, ALU.mult, ALU.add))
                rsqrt(2).then_inc(inv_ready, 1)
                dve.wait_ge(inv_ready, st.norms + 1)
                dve.tensor_scalar(xs[:, 0, :], x[:, 0, :], stat[:, 2, 0:1], None, ALU.mult).then_inc(xs_dve, 1)

            def operand(st):
                if st.src == "features":
                    for b in range(4):
                        dve.wait_ge(op_hi, st.operand + b + 1)
                        f = slice(2 * b, 2 * b + 2)
                        dve.tensor_tensor(xT_lo[:, f, :], features[:, f, :], xT_hi[:, f, :].bitcast(F32), ALU.subtract
                                          ).then_inc(op_lo, 1)
                    return
                for b in range(-(-st.kts // 2)):
                    dve.wait_ge(op_hi, st.operand + b + 1)
                    for k in range(2 * b, min(2 * b + 2, st.kts)):
                        src = bank[:, 4 + b, (k % 2) * S:(k % 2 + 1) * S]
                        g = 1.0 if st.gain is None else gain(st.gain, 0 if "subln" in st.gain else k)
                        last = dve.scalar_tensor_tensor(xT_lo[:, k, :], src, g, xT_hi[:, k, :].bitcast(F32),
                                                        ALU.mult, ALU.subtract)
                    last.then_inc(op_lo, 1)

            def rotate(v, half, cos, sin, c1, c2):
                shape = list(v.shape)
                cb = cos.rearrange("p (t r) -> p t r", t=T2).unsqueeze(2).broadcast_to(shape)
                sb_ = sin.rearrange("p (t r) -> p t r", t=T2).unsqueeze(2).broadcast_to(shape)
                dve.tensor_tensor(c1, v, cb, ALU.mult)
                dve.tensor_tensor(c2[:, :, :, 0:half], v[:, :, :, half:], sb_[:, :, :, 0:half], ALU.mult)
                return dve.tensor_tensor(c2[:, :, :, half:], v[:, :, :, 0:half], sb_[:, :, :, half:], ALU.mult)

            def turned_low(dst_hi, dst_lo, b, split, first_bank=6, parts=P):
                dve.wait_ge(split_hi, split)
                src = bank[0:parts, first_bank:first_bank + 2, :].rearrange("p b n -> p (b n)")
                dve.tensor_tensor(block_part(dst_lo, b, 4), src.rearrange("p (f n) -> p f n", n=S),
                                  block_part(dst_hi, b, 4).bitcast(F32), ALU.subtract).then_inc(split_lo, 1)

            def values_low(src, hi, lo_):
                dve.tensor_tensor(lo_, src, hi.bitcast(F32), ALU.subtract).then_inc(values_lo, 1)

            def qkv_block(at, s0, r0, split, b, check, parts, rope=True, meanwhile=lambda s: None):
                q, k, v = parts
                for s in range(3):
                    lo(at + (2 * s + LEAD))
                    lo(at + (2 * s + LEAD + 1))
                    meanwhile(s)
                    if s < 2 and rope:
                        dve.wait_ge(slab_out, s0 + (s + 1))
                        if check or s:
                            dve.wait_ge(rope_done, r0 + s)
                        w = stage[:, s, :, :].rearrange("p t (h d) -> p t h d", d=64)[:, :, :, 0:16]
                        c1 = rot[:, 0, :].rearrange("p (t h d) -> p t h d", t=T2, d=16)
                        c2 = rot[:, 1, :].rearrange("p (t h d) -> p t h d", t=T2, d=16)
                        rotate(w, 8, const_ap("cos_a"), const_ap("sin_a"), c1, c2).then_inc(rope_mul, 1)
                        dve.wait_ge(rope_mul, r0 + (s + 1))
                        dve.tensor_tensor(w, c1, c2, ALU.add).then_inc(rope_done, 1)
                    if s == 2:
                        dve.wait_ge(slab_out, s0 + 3)
                        values_low(bank[:, 4:6, :], block_part(v[0], b, 1).rearrange("p a t n -> p (a t) n"),
                                   block_part(v[1], b, 1).rearrange("p a t n -> p (a t) n"))
                    if s >= 1:
                        hi, low = (q, k)[s - 1]
                        turned_low(hi, low, b, split + s)

            def qkv(st):
                parts = operands("A")
                if st.slab == 0:
                    for b in range(st.groups):
                        qkv_block(Place(st.tile + 6 * b), st.slab + 3 * b, st.rope + 2 * b, st.split + 2 * b, b,
                                  b > 0, parts)
                else:
                    with dve.Fori(0, st.groups) as b:
                        qkv_block(Place(st.tile, b * 2), b * 3 + st.slab, b * 2 + st.rope, b * 2 + st.split, b,
                                  True, parts)

            def turn_heads(st):
                for i in range(4):
                    turned_low((QB_hi, KB_hi)[i // 2], (QB_lo, KB_lo)[i // 2], i % 2, st.split + i + 1,
                               4 + 2 * (i % 2), 96)

            def latent(st):
                for i in range(3):
                    lo(Place(st.tile + i + LEAD))
                dve.wait_ge(slab_out, st.slab + 2)
                parts = [(0, 384), (384, 640)]
                for i, (a, b) in enumerate(parts):
                    for t in range(T2):
                        last = square_sum(a_tm[:, t, a:b], b - a, 2 * i + t, xs[:, t, a:b])
                link(last)
                for i, (a, b) in enumerate(parts):
                    last = dve.tensor_scalar(stat[:, 1, 2 * i:2 * i + 2], stat[:, 0, 2 * i:2 * i + 2], 1.0 / (b - a),
                                             EPS, ALU.mult, ALU.add)
                link(last)
                link(rsqrt(4))
                kr = a_tm[:, :, 640:672].unsqueeze(2)
                c1 = rot[:, 0, 0:64].rearrange("p (t h d) -> p t h d", t=T2, h=1)
                c2 = rot[:, 1, 0:64].rearrange("p (t h d) -> p t h d", t=T2, h=1)
                link(rotate(kr, 16, const_ap("cos_b"), const_ap("sin_b"), c1, c2))
                dve.tensor_tensor(kr, c1, c2, ALU.add)
                for i, (a, b) in enumerate(parts):
                    for t in range(T2):
                        last = dve.tensor_scalar(a_tm[:, t, a:b], a_tm[:, t, a:b],
                                                 stat[:, 2, 2 * i + t:2 * i + t + 1], None, ALU.mult)
                last.then_inc(lat_ready, 1)
                dve.wait_ge(lat_ready, 1)

            def lift(st):
                for i in range(3):
                    lo(Place(st.tile + i + LEAD))
                dve.wait_ge(slab_out, st.slab + 3)
                v = q_tm[:, :, :].rearrange("p t (h d) -> p t h d", d=96)[:, :, :, 64:96]
                c1 = xs[:, 0, :].rearrange("p (t h d) -> p t h d", t=T2, d=32)
                c2 = xs[:, 1, :].rearrange("p (t h d) -> p t h d", t=T2, d=32)
                link(rotate(v, 16, const_ap("cos_b"), const_ap("sin_b"), c1, c2))
                dve.tensor_tensor(v, c1, c2, ALU.add).then_inc(lat_ready, 1)
                lo(Place(st.tile + 3 + LEAD))
                k4 = k_tm[:, :, :].rearrange("p t (h d) -> p t h d", d=96)
                for t in range(T2):
                    last = dve.tensor_copy(k4[:, t, :, 64:96],
                                           a_tm[:, t, 640:672].unsqueeze(1).broadcast_to([P, 16, 32]))
                last.then_inc(lat_ready, 1)
                lo(Place(st.tile + 4 + LEAD))
                for i in range(2):
                    dve.wait_ge(slab_out, st.slab + 6 + i)
                    c = slice(i * BANK, (i + 1) * BANK)
                    p = 2 * ((5 + i) % 3)
                    values_low(bank[:, p:p + 2, :], VB_hi[:, :, c], VB_lo[:, :, c])

            def attend(st, beside=lambda u: None):
                units = unit_list(st)
                n, U = len(units), st.unit
                d = P if st.mix == "A" else 64
                per = BANK // d

                def maximum(u):
                    dve.wait_ge(scores, U + u + 1)
                    if u >= 2:
                        dve.wait_ge(exped, U + u - 1)
                    h, t = units[u]
                    if st.mix in "AB":
                        subs = 2 if st.mix == "A" else 1
                        src = bank[:, 2 * (u % 2):2 * (u % 2) + subs, 0:S]
                        dve.tensor_reduce(nmax[:, u % 2, 0:subs], src, AX_X, ALU.max, negate=True).then_inc(maxed, 1)
                        return
                    if u >= 2:
                        dve.wait_ge(probs_turned, U + u - 1)
                    w = 768 if st.mix == "C" else S
                    b = 2 * (u % 2)
                    src = bank[:, b:b + 2, :].rearrange("p b n -> p (b n)")[:, 0:w]
                    o = (t * S if st.mix == "C" else (1 - t) * P)
                    m = const_ap("mask" if st.mix == "C" else "causal")[:, o:o + w]
                    link(dve.tensor_tensor_reduce(out=probs[:, u % 2, 0:w], in0=src, in1=m, scale=1.0, scalar=LOWEST,
                                                  op0=ALU.add, op1=ALU.max, accum_out=nmax[:, u % 2, 1:2]))
                    dve.tensor_scalar(nmax[:, u % 2, 0:1], nmax[:, u % 2, 1:2], -1.0, None, ALU.mult
                                      ).then_inc(maxed, 1)

                def mix(u):
                    dve.wait_ge(exped, U + u + 1)
                    r = stat[:, 4, 0:1]
                    link(dve.reciprocal(r, sums[:, 1, u:u + 1]))
                    link(dve.scalar_tensor_tensor(stat[:, 4, 1:2], r, sums[:, 0, u:u + 1], lam[:, st.j:st.j + 1],
                                                  ALU.mult, ALU.mult))
                    dve.scalar_tensor_tensor(probs[:, u % 2, 0:S], probs[:, u % 2, S:2 * S], stat[:, 4, 1:2],
                                             probs[:, u % 2, 0:S], ALU.mult, ALU.add).then_inc(mixed, 1)

                def copy_turned(u):
                    dve.wait_ge(pt_hi, U + u + 1)
                    free = buffer_free(st, u)
                    if free is not None:
                        dve.wait_ge(o_done, free)
                    tb = turned_buffer(st, u)
                    n_ = 6 if st.mix == "C" else 2
                    b = turn_banks(st, u)[0]
                    src = bank[:, b:b + 2, :].rearrange("p b n -> p (b n)")[:, 0:n_ * P] if n_ > 4 \
                        else bank[:, b, 0:n_ * P]
                    dve.tensor_tensor(probsT_lo[:, tb, 0:n_, :], src.rearrange("p (k q) -> p k q", q=P),
                                      probsT_hi[:, tb, 0:n_, :].bitcast(F32), ALU.subtract).then_inc(pt_lo, 1)

                def result(b):
                    dve.wait_ge(o_done, U + (b + 1) * per)
                    inv = stat[:, 4, 8:8 + per]
                    link(dve.reciprocal(inv, sums[:, 0, b * per:(b + 1) * per]))
                    hs = per // 2
                    w = hs * d
                    w0 = b * w + (st.j * BANK if st.mix in "BC" else 0)
                    o = xs[:, :, w0:w0 + w].rearrange("p t (h d) -> p h t d", d=d)
                    src = bank[:, 6 + (0 if st.mix == "M" else b % 2), :].rearrange("p (h t d) -> p h t d", t=T2, d=d)
                    dve.tensor_tensor(o, src, inv.rearrange("p (h t) -> p h t", t=T2).unsqueeze(3)
                                      .broadcast_to([P, hs, T2, d]), ALU.mult).then_inc(o_out, 1)

                def feature_result(b):
                    dve.wait_ge(o_done, U + 8 * (b + 1))
                    f = st.j * 4 + 2 * b
                    for odd in range(2):
                        dve.tensor_copy(features[odd * 64:odd * 64 + 64, f:f + 2, :],
                                        bank[0:64, 6 + odd, :].rearrange("p (f n) -> p f n", n=S)).then_inc(o_out, 1)

                maximum(0)
                if by_feature(st):
                    for u in range(n + 1):
                        if u < n:
                            dve.wait_ge(exped, U + u + 1)
                            dve.reciprocal(sums[:, 1, u:u + 1], sums[:, 0, u:u + 1]).then_inc(inv_sums, 1)
                        if u + 1 < n:
                            maximum(u + 1)
                        if u >= 1:
                            copy_turned(u - 1)
                        if u == 10:
                            feature_result(0)
                    feature_result(1)
                    return
                for u in range(n + 1):
                    if st.mix == "A":
                        if u < n:
                            mix(u)
                        if u + 1 < n:
                            maximum(u + 1)
                        if u >= 1:
                            copy_turned(u - 1)
                        if u % per == 2 and u >= 6:
                            result(u // per - 1)
                    elif u < n:
                        if u + 1 < n:
                            maximum(u + 1)
                        copy_turned(u)
                        if u % per == 0 and u:
                            result(u // per - 1)
                        beside(u)
                result(n // per - 1)
                if st.mix == "A":
                    dve.wait_ge(o_sq, 4 * (st.j + 1))
                    link(dve.tensor_scalar(stat[:, 1, 0:16], stat[:, 0, 0:16], 1.0 / P, EPS, ALU.mult, ALU.add))
                    link(rsqrt(16))
                    v = xs[:, :, :].rearrange("p t (h d) -> p (t h) d", d=P)
                    dve.tensor_tensor(v, v, stat[:, 2, 0:16].unsqueeze(2).broadcast_to([P, 16, P]), ALU.mult
                                      ).then_inc(xs_dve, 1)

            def inverse_rms(width):
                link(dve.tensor_scalar(stat[:, 1, 0:2], stat[:, 0, 0:2], 1.0 / width, EPS, ALU.mult, ALU.add))
                link(rsqrt(2))

            def final_norm(st):
                for t in range(T2):
                    last = square_sum(x[:, t, :], D, t, xs[:, t, :])
                link(last)
                inverse_rms(D)
                dve.wait_ge(row_in, 16)
                for t in range(T2):
                    last = dve.scalar_tensor_tensor(x[:, t, :], x[:, t, :], stat[:, 2, t:t + 1], row[:, :],
                                                    ALU.mult, ALU.mult)
                last.then_inc(row_used, 1)
                dve.wait_ge(row_used, 1)
                dve.sem_inc(x_ready, 1)

            def wrap(dst, src, tmp, add=0.0, scale=1.0):
                link(dve.tensor_scalar(dst, src, scale, add, ALU.mult, ALU.add))
                link(dve.tensor_scalar(tmp, dst, MAGIC, None, ALU.add))
                link(dve.tensor_scalar(tmp, tmp, MAGIC, None, ALU.subtract))
                link(dve.tensor_tensor(dst, dst, tmp, ALU.subtract))

            def poles(st):
                dt, ad, mag, ang, tmp, cr, ci, den, nr, li, m2, t3 = (pole[:, i, :] for i in range(12))
                re, im = gains("a_re"), gains("a_im")
                dve.wait_ge(dt_ready, 1)
                dve.tensor_tensor(ad, re, dt, ALU.mult).then_inc(mag_ready, 1)
                link(dve.tensor_tensor(ang, im, dt, ALU.mult))
                link(dve.tensor_scalar(tmp, ang, 1.0 / TURN, MAGIC, ALU.mult, ALU.add))
                link(dve.tensor_scalar(tmp, tmp, MAGIC, None, ALU.subtract))
                link(dve.scalar_tensor_tensor(ang, tmp, -TURN_HI, ang, ALU.mult, ALU.add))
                link(dve.scalar_tensor_tensor(ang, tmp, -TURN_LO, ang, ALU.mult, ALU.add))
                wrap(trig[:, 0, 0, :], ang, tmp, scale=1.0 / TURN)
                for k in range(1, SHIFTS):
                    wrap(trig[:, 0, k, :], trig[:, 0, k - 1, :], tmp, scale=2.0)
                sines = trig[:, 0, :, :].rearrange("p k n -> p (k n)")
                cosines = trig[:, 1, :, :].rearrange("p k n -> p (k n)")
                wrap(cosines, sines, E_re[:, 0, 0:SHIFTS * STILES], add=0.25)
                link(dve.tensor_scalar(trig[:, :, :, :], trig[:, :, :, :], 0.4999999, -0.4999999, ALU.min, ALU.max))
                dve.sem_inc(angle_ready, 1)
                dve.wait_ge(trig_ready, 1)
                dve.wait_ge(dt_ready, 2)
                link(dve.tensor_tensor(nr, mag, trig_k[:, 1, 0, :], ALU.mult))
                dve.tensor_scalar(nr, nr, -1.0, None, ALU.add)
                dve.tensor_tensor(li, mag, trig_k[:, 0, 0, :], ALU.mult)
                dve.tensor_tensor(den, re, re, ALU.mult)
                link(dve.tensor_tensor(m2, im, im, ALU.mult))
                link(dve.tensor_tensor(den, den, m2, ALU.add))
                link(dve.reciprocal(den, den))
                dve.tensor_tensor(cr, nr, re, ALU.mult)
                dve.tensor_tensor(m2, li, im, ALU.mult)
                dve.tensor_tensor(ci, li, re, ALU.mult)
                link(dve.tensor_tensor(t3, nr, im, ALU.mult))
                dve.tensor_tensor(cr, cr, m2, ALU.add)
                link(dve.tensor_tensor(ci, ci, t3, ALU.subtract))
                dve.tensor_tensor(cr, cr, den, ALU.mult)
                link(dve.tensor_tensor(ci, ci, den, ALU.mult))

            def output_factors():
                dve.wait_ge(s5_in_done, 16)
                shape = [P, STILES, 32]
                cr = pole[:, 5, :].unsqueeze(2).broadcast_to(shape)
                ci = pole[:, 6, :].unsqueeze(2).broadcast_to(shape)
                a, b = (xs[:, 0, i * BANK:(i + 1) * BANK].rearrange("p (n h) -> p n h", h=32) for i in range(2))
                dve.tensor_tensor(a, C_in[:, 0, :, :], cr, ALU.mult)
                link(dve.tensor_tensor(b, C_in[:, 1, :, :], ci, ALU.mult))
                link(dve.tensor_tensor(Cc[:, 0, :, :], a, b, ALU.subtract))
                dve.tensor_tensor(a, C_in[:, 0, :, :], ci, ALU.mult)
                link(dve.tensor_tensor(b, C_in[:, 1, :, :], cr, ALU.mult))
                dve.scalar_tensor_tensor(Cc[:, 1, :, :], a, -1.0, b, ALU.mult, ALU.subtract).then_inc(pole_ready, 1)

            def phase_tables(k):
                n = 2 ** k
                shape = [P, STILES, n]
                c = trig_k[:, 1, k, :].unsqueeze(2).broadcast_to(shape)
                s_ = trig_k[:, 0, k, :].unsqueeze(2).broadcast_to(shape)
                tmp = xs[:, :, :].rearrange("p t d -> p (t d)")[:, 0:STILES * n].rearrange("p (i n) -> p i n", i=STILES)
                old_r, old_i = E_re[:, :, 0:n], E_im[:, :, 0:n]
                new_r, new_i = E_re[:, :, n:2 * n], E_im[:, :, n:2 * n]
                dve.tensor_tensor(new_r, old_r, c, ALU.mult)
                link(dve.tensor_tensor(tmp, old_i, s_, ALU.mult))
                link(dve.tensor_tensor(new_r, new_r, tmp, ALU.subtract))
                dve.tensor_tensor(new_i, old_i, c, ALU.mult)
                link(dve.tensor_tensor(tmp, old_r, s_, ALU.mult))
                link(dve.tensor_tensor(new_i, new_i, tmp, ALU.add))

            def hybrid_layer(st):
                at = Place(st.tile)
                poles(st)
                lo(at + LEAD)
                output_factors()
                dve.memset(E_re[:, :, 0:1], 1.0)
                link(dve.memset(E_im[:, :, 0:1], 0.0))
                for k in range(5):
                    phase_tables(k)
                lo(at + (LEAD + 1))
                qkv_block(at + 2, st.slab + 1, None, st.split, 0, True, operands("M"), rope=False,
                          meanwhile=lambda s: phase_tables(5 + s))

                def to_states(i):
                    er = E_re[:, i, :].unsqueeze(1).broadcast_to([P, 2, S])
                    ei = E_im[:, i, :].unsqueeze(1).broadcast_to([P, 2, S])
                    v = bank[:, 1 + 2 * (i % 2), :].rearrange("p (c n) -> p c n", c=2)
                    dve.wait_ge(v_done, i + 1)
                    if i >= 1:
                        dve.wait_ge(scanned, i)
                    if i >= 2:
                        dve.wait_ge(states, i - 1)
                    dve.tensor_tensor(pre_c[:, :, :], v, er, ALU.mult)
                    dve.tensor_tensor(pre_s[:, :, :], v, ei, ALU.mult).then_inc(v_used, 1)
                    dve.wait_ge(v_used, i + 1)
                    dve.tensor_tensor(pre_c[:, 0, :], pre_c[:, 0, :], pre_s[:, 1, :], ALU.add)
                    link(dve.tensor_tensor(pre_c[:, 1, :], pre_c[:, 1, :], pre_s[:, 0, :], ALU.subtract))
                    radius = pole[:, 2, i:i + 1].broadcast_to([P, S])
                    for c in range(2):
                        last = dve.tensor_tensor_scan(scan[:, i % 2, c, :], radius, pre_c[:, c, :], 0.0,
                                                      ALU.mult, ALU.add)
                    last.then_inc(scanned, 1)

                def outputs(f):
                    dve.wait_ge(y_done, 4 * f + 4)
                    dve.scalar_tensor_tensor(y_skip[:, f, :], uT[:, f, :], gain("ssm_d", f),
                                             bank[:, 5 + 2 * (f % 2), 0:S], ALU.mult, ALU.add).then_inc(y_out, 1)

                def beside(u):
                    to_states(u)
                    if u >= 7 and u % 4 == 3:
                        outputs(u // 4 - 1)

                attend(st, beside)
                outputs(3)
                dve.wait_ge(gelu_done, 1)
                dve.wait_ge(glu_hi, 1)
                dve.tensor_tensor(xT_lo[:, 0:4, :], y_act[:, :, :], xT_hi[:, 0:4, :].bitcast(F32), ALU.subtract
                                  ).then_inc(glu_lo, 1)
                lo(at + (8 + LEAD))
                for t in range(T2):
                    last = square_sum(xs[:, t, 0:BANK], BANK, t, xs[:, t, BANK:])
                link(last)
                inverse_rms(BANK)
                for t in range(T2):
                    last = dve.tensor_scalar(xs[:, t, 0:BANK], xs[:, t, 0:BANK], stat[:, 2, t:t + 1], None, ALU.mult)
                last.then_inc(hybrid_xs, 1)
                dve.wait_ge(sig_done, 1)
                link(dve.tensor_tensor(y_gated[:, :, :], y_act[:, :, :], sig[:, :, :], ALU.mult))
                dve.tensor_tensor(y_sq[:, :, :], y_gated[:, :, :], y_gated[:, :, :], ALU.mult).then_inc(sq_done, 1)
                for b in range(2):
                    dve.wait_ge(op_hi, st.operand + b + 1)
                    for k in (2 * b, 2 * b + 1):
                        last = dve.scalar_tensor_tensor(xT_lo[:, 4 + k, :], bank[:, 4 + b, (k % 2) * S:(k % 2 + 1) * S],
                                                        gain("attn_out", k), xT_hi[:, 4 + k, :].bitcast(F32),
                                                        ALU.mult, ALU.subtract)
                    last.then_inc(op_lo, 1)
                dve.wait_ge(ss_done, 1)
                link(dve.tensor_scalar(inv3[:, 0, :], bank[:, 2, 0:S], 1.0 / BANK, EPS, ALU.mult, ALU.add))
                link(rsqrt(S, inv3))
                dve.tensor_tensor(y_norm[:, :, :], y_gated[:, :, :],
                                  inv3[:, 1, :].unsqueeze(1).broadcast_to([P, 4, S]), ALU.mult).then_inc(norm_done, 1)
                dve.wait_ge(mix_hi, 1)
                for k in range(4):
                    last = dve.scalar_tensor_tensor(xT_lo[:, k, :], y_norm[:, k, :], gain("ssm_out", k),
                                                    xT_hi[:, k, :].bitcast(F32), ALU.mult, ALU.subtract)
                last.then_inc(mix_lo, 1)

            def residual(st, last_tile):
                dve.wait_ge(w_used, last_tile + 1 + RING)
                if st.post:
                    for t in range(T2):
                        last = dve.tensor_copy(xs[:, t, :], bank[:, 2 * t:2 * t + 2, :].rearrange("p b n -> p (b n)"))
                    link(last)
                    for t in range(T2):
                        last = square_sum(xs[:, t, :], D, t, h_junk[:, t, :])
                    link(last)
                    inverse_rms(D)
                    dve.wait_ge(row_in, 16 * (st.rows + 1))
                    for t in range(T2):
                        last = dve.scalar_tensor_tensor(xs[:, t, :], xs[:, t, :], stat[:, 2, t:t + 1], row[:, :],
                                                        ALU.mult, ALU.mult)
                    last.then_inc(row_used, 1)
                    dve.wait_ge(row_used, st.rows + 1)
                    for t in range(T2):
                        last = dve.tensor_tensor(x[:, t, :], xs[:, t, :], x[:, t, :], ALU.add)
                    last.then_inc(x_ready, 1)
                    dve.wait_ge(x_ready, st.x_ready + 1)
                    return
                for t in range(T2):
                    last = dve.tensor_tensor(x[:, t, :], bank[:, 2 * t:2 * t + 2, :].rearrange("p b n -> p (b n)"),
                                             x[:, t, :], ALU.add)
                last.then_inc(x_ready, 1)
                dve.wait_ge(x_ready, st.x_ready + 1)

            def out_projection(st):
                for i in range(4):
                    lo(Place(st.tile + i + LEAD))
                residual(st, st.tile + 3)

            def ffn(st):
                C, J = st.chunk, st.pair

                def hidden(at, c, c_mod, p):
                    dve.wait_ge(silu_done, c + 1)
                    dve.tensor_tensor(h32[:, p, c_mod % 2, :], bank[:, 4 + c_mod, S:2 * S], sg[:, c_mod % 2, :],
                                      ALU.mult).then_inc(h_done, 1)

                def pair(at, c, j, p, three=True):
                    lo(at + LEAD)
                    hidden(at, c, 2 * p, p)
                    lo(at + (LEAD + 1))
                    hidden(at + 1, c + 1, 2 * p + 1, p)
                    if three:
                        lo(at + (LEAD + 2))
                    dve.wait_ge(h_hi, j + 1)
                    dve.tensor_tensor(hT_lo[:, p, :, :], h32[:, p, :, :], hT_hi[:, p, :, :].bitcast(F32),
                                      ALU.subtract).then_inc(h_lo, 1)

                at = Place(st.tile)
                pair(at, C, J, 0, False)
                pair(at + 2, C + 2, J + 1, 1)
                pair(at + 5, C + 4, J + 2, 0)
                with dve.Fori(0, 3) as i:
                    for p in range(2):
                        pair(Place(st.tile + 8 + 3 * p, i * 2), i * 4 + (C + 6 + 2 * p), i * 2 + (J + 3 + p),
                             (1 + p) % 2)
                for p in range(2):
                    pair(at + (26 + 3 * p), C + 18 + 2 * p, J + 9 + p, (1 + p) % 2)
                lo(at + (32 + LEAD))
                residual(st, st.tile + 32)

            for n in range(LEAD):
                lo(Place(n))
            dve.wait_ge(small_in, 48)
            v = lam_raw[:, 0:512].rearrange("p (w s n) -> p w s n", w=2, s=2)
            prod = lam_raw[:, 512:768].rearrange("p (w n) -> p w n", w=2)
            link(dve.tensor_tensor(prod, v[:, :, 0, :], v[:, :, 1, :], ALU.mult))
            dve.tensor_reduce(lam[:, 4:8], lam_raw[:, 512:768].rearrange("p (a n) -> p a n", n=64), AX_X, ALU.add
                              ).then_inc(lam_dots, 1)
            dve.wait_ge(lam_exp, 1)
            link(dve.tensor_tensor(lam[:, 0:2], lam[:, 10:12], lam[:, 8:10], ALU.subtract))
            for j in range(2):
                dve.tensor_scalar(lam[:, j:j + 1], lam[:, j:j + 1], -lambda_init(3 * j), None, ALU.add)
                g = gain(f"subln{j}", 0)
                last = dve.tensor_scalar(g, g, 1.0 - lambda_init(3 * j), None, ALU.mult)
            link(last)
            for st in stages:
                {"operand": operand, "qkv": qkv, "latent": latent, "lift": lift, "turn": turn_heads,
                 "attend": attend, "out": out_projection, "ffn": ffn, "norm": norm, "fetch": lambda s: None,
                 "final_norm": final_norm, "hybrid": hybrid_layer}[st.kind](st)
            dve.sem_inc(out_ready, 1)


def constants():
    c = np.zeros((P, CONST_W), np.float32)

    def put(name, v):
        o, w = CONST[name]
        c[:, o:o + w] = v.reshape(P, w)

    put("ones", np.ones((P, P), np.float32))
    put("ident", np.eye(P, dtype=np.float32))
    for name, rot in (("a", 16), ("b", 32)):
        pos = np.arange(S, dtype=np.float32)
        inv = np.float32(500000.0) ** (-np.arange(0, rot, 2, dtype=np.float32) / np.float32(rot))
        ang = (pos[:, None] * inv[None, :].astype(np.float32)).astype(np.float32)
        cos, sin = np.cos(ang), np.sin(ang)
        put(f"cos_{name}", np.concatenate([cos, cos], 1).reshape(T2, P, rot).transpose(1, 0, 2))
        put(f"sin_{name}", np.concatenate([-sin, sin], 1).reshape(T2, P, rot).transpose(1, 0, 2))
    i = np.arange(P)[:, None]
    k = np.arange(S)[None, :]
    off = np.float32(-1e30)

    def mask(keep):
        return np.where(keep, np.float32(0.0), off)

    put("mask", np.concatenate([mask(abs(i - k) <= 64), mask((i - k) % 4 == 0), mask((i - k) % 16 == 0),
                                mask(abs(i + P - k) <= 64)], 1))
    put("causal", mask(np.arange(384)[None, :] <= i + P))
    return c


def put_tiles(tape, at, block):
    tape[at:at + block.shape[0], :, :block.shape[2]] = block
    return at + block.shape[0]


def slabs(w):
    n = w.shape[1] // BANK
    return w.reshape(2, 4, P, n, BANK).transpose(3, 0, 2, 1, 4).reshape(2 * n, P, 4 * BANK)


def blocks(w, groups, order):
    n = w.shape[1] // (3 * BANK * groups)
    v = w.reshape(D, groups, 3, n, BANK)
    v = v.transpose(0, 3, 1, 2, 4) if order == "halves" else v.transpose(0, 1, 3, 2, 4)
    return slabs(np.ascontiguousarray(v).reshape(D, -1))


def out_tiles(w):
    return w.reshape(-1, 2, P, D).transpose(0, 2, 1, 3).reshape(-1, P, 2 * D)


def put_ffn(tape, at, gate, up, down):
    gu = np.stack([gate, up], 1).reshape(KD, P, 2, CHUNKS, P).transpose(3, 1, 0, 2, 4).reshape(CHUNKS, P, TILE)
    dn = out_tiles(down)
    order = [gu[0], gu[1]]
    for j in range(1, CHUNKS // 2):
        order += [gu[2 * j], gu[2 * j + 1], dn[j - 1]]
    order.append(dn[-1])
    for t in order:
        tape[at] = t
        at += 1
    return at


def layout(w):
    tape = np.zeros((plan()[1], P, TILE), np.float32)
    at = 0
    for layer in LAYERS:
        j = layer // 3
        if layer % 3 == 0:
            at = put_tiles(tape, at, blocks(w["a_w_qkv"][j], 1, "groups"))
            at = put_tiles(tape, at, out_tiles(w["a_w_o"][j]))
        elif layer % 3 == 1:
            a = w["b_w_a"][j]
            at = put_tiles(tape, at, slabs(a[:, :BANK]))
            at = put_tiles(tape, at, a[:, BANK:].reshape(1, KD, P, 160).transpose(0, 2, 1, 3).reshape(1, P, KD * 160))
            at = put_tiles(tape, at, w["b_w_qb"][j].reshape(3, P, 3, BANK).transpose(2, 1, 0, 3).reshape(3, P, 3 * BANK))
            kv = w["b_w_kvb"][j].reshape(2, P, 16, 2, 64).transpose(3, 1, 0, 2, 4).reshape(2, P, 2 * D)
            at = put_tiles(tape, at, kv)
            at = put_tiles(tape, at, out_tiles(w["b_w_o"][j]))
        else:
            at = put_tiles(tape, at, blocks(w["c_w_qkv"][j], 3, "halves"))
            at = put_tiles(tape, at, out_tiles(w["c_w_o"][j]))
        gu = w["f_w_gu"][layer]
        at = put_ffn(tape, at, gu[:, :FFN], gu[:, FFN:], w["f_w_out"][layer])
    at = put_tiles(tape, at, slabs(w["w_in_2"][0]))
    at = put_tiles(tape, at, w["w_glu_2"][0].reshape(1, 4, P, BANK).transpose(0, 2, 1, 3).reshape(1, P, 4 * BANK))
    at = put_tiles(tape, at, out_tiles(w["w_out_2"][0]))
    at = put_ffn(tape, at, w["w_gate_2"][0], w["w_up_2"][0], w["w_down_2"][0])
    assert at == tape.shape[0]
    small = np.zeros((P, SMALL_W), np.float32)

    def col(name, v):
        o, width = SMALL[name]
        small[:, o:o + width] = v.reshape(width, P).T

    for layer in range(4):
        col(f"attn_norm{layer}", w["attn_norm"][layer])
        col(f"ffn_norm{layer}", w["ffn_norm"][layer])
    col("lat", np.concatenate([w["b_q_norm"][0], w["b_kv_norm"][0]]))
    for j in range(2):
        col(f"subln{j}", w["a_subln"][j])
    col("pre_mix", w["g_pre_mix_2"][0])
    col("pre_ffn", w["g_pre_ffn_2"][0])
    col("ssm_out", w["g_ssm_out_2"][0])
    col("attn_out", w["g_attn_out_2"][0])
    col("b_glu", w["b_glu_2"][0])
    col("ssm_d", w["ssm_d_2"][0])
    col("a_re", w["ssm_a_re_2"][0])
    col("a_im", w["ssm_a_im_2"][0])
    col("log_dt", np.repeat(w["ssm_log_dt_2"][0], STATES))
    s5 = np.zeros((P, S5_W), np.float32)
    b_in = s5[:, :1024].reshape(P, 2, 4, P)
    c_in = s5[:, 1024:].reshape(P, 2, STILES, 32)
    for c, name in enumerate(("re", "im")):
        b, cc = w[f"ssm_b_{name}_2"][0], w[f"ssm_c_{name}_2"][0]
        for g in range(GROUPS):
            i, odd = divmod(g, 2)
            f = (i % 4) * 32 + odd * GIN
            b_in[f:f + GIN, c, i // 4, odd * STATES:(odd + 1) * STATES] = b[g].T
            c_in[odd * STATES:(odd + 1) * STATES, c, i, odd * GIN:(odd + 1) * GIN] = cc[g].T
    return tape, small, s5


def kernel(**inputs):
    import concourse.bacc as bacc
    from concourse.bass_utils import run_bass_kernel_spmd

    w = {n: np.asarray(v) for n, v in inputs.items()}
    tape, small, s5 = layout(w)
    lam = np.concatenate([w[f"a_lambda_{n}"].reshape(-1) for n in ("q1", "k1", "q2", "k2")])
    arrays = {"x_dram": w["x"][0], "tape_dram": tape, "small_dram": small, "const_dram": constants(),
              "lam_dram": lam, "rows_dram": np.stack([w["final_norm"], w["g_post_mix_2"][0], w["g_post_ffn_2"][0]]), "s5_dram": s5}
    nc = bacc.Bacc("TRN2", target_bir_lowering=False, num_devices=1, dynamic_dma_scratch_size=1024)
    args = [nc.dram_tensor(n, a.shape, F32, kind="ExternalInput").ap() for n, a in arrays.items()]
    out = nc.dram_tensor("out_dram", (S, D), F32, kind="ExternalOutput").ap()
    build_program(nc, *args, out)
    r = run_bass_kernel_spmd(nc, [arrays], core_ids=[0])
    return r.results[0]["out_dram"].reshape(1, S, D)
```
